# Optimizing a Trainium2 kernel written in Bass

```python
import jax, jax.numpy as jnp
from jax import lax
import numpy as np

D_MODEL = 2048
BATCH = 1
SEQ = 256
DEPTH = 2

N_MIXERS = 2
N_SC_LAYERS = (DEPTH + 1) // 2
N_SSD_LAYERS = DEPTH // 2
SC_CONV = 3
SSM_EXPAND = 2
D_INNER = SSM_EXPAND * D_MODEL
HEAD_DIM = 64
N_SSM_HEADS = D_INNER // HEAD_DIM
D_STATE = 128
N_GROUPS = 8
SSM_CONV = 3
CHUNK = 128
CONV_DIM = D_INNER + 2 * N_GROUPS * D_STATE
IN_PROJ_DIM = D_INNER + CONV_DIM + 2 * N_SSM_HEADS
D_FF = 4 * D_MODEL
EPS = 1e-6

kernel_name = "hybrid_shortconv_ssd_adaln_encoder"

def rms_norm(x, g):
    xf = x.astype(jnp.float32)
    y = xf * lax.rsqrt(jnp.mean(xf * xf, axis=-1, keepdims=True) + EPS)
    return (y * g.astype(jnp.float32)).astype(x.dtype)

def dwconv_centred(u, w):
    k = w.shape[1]
    pad = k // 2
    kern = jnp.transpose(w)[:, None, :].astype(u.dtype)
    return lax.conv_general_dilated(u, kern, window_strides=(1,), padding=[(pad, pad)],
                                    dimension_numbers=('NWC', 'WIO', 'NWC'),
                                    feature_group_count=u.shape[-1])

def short_conv_mixer(h, w_in, w_conv, w_out):
    b_gate, c_gate, v = jnp.split(h @ w_in, 3, axis=-1)
    u = dwconv_centred(c_gate * v, w_conv)
    return (b_gate * u) @ w_out

def ssd_chunked(x, dt, a_neg, bm, cm):
    b, L, H, P = x.shape
    G, N = bm.shape[2], bm.shape[3]
    R = H // G
    nc = L // CHUNK
    f32 = jnp.float32
    xs = jnp.moveaxis(x.astype(f32).reshape(b, nc, CHUNK, G, R, P), 1, 0)
    dts = jnp.moveaxis(dt.reshape(b, nc, CHUNK, G, R), 1, 0)
    av = dts * a_neg.reshape(G, R)
    bs = jnp.moveaxis(bm.astype(f32).reshape(b, nc, CHUNK, G, N), 1, 0)
    cs = jnp.moveaxis(cm.astype(f32).reshape(b, nc, CHUNK, G, N), 1, 0)
    mask = jnp.tril(jnp.ones((CHUNK, CHUNK), dtype=bool))[None, :, :, None, None]

    def step(state, inp):
        xc, ac, dtc, bc, cc = inp
        cum = jnp.cumsum(ac, axis=1)
        seg = cum[:, :, None] - cum[:, None, :]
        decay = jnp.exp(jnp.where(mask, seg, -jnp.inf))
        scores = jnp.einsum('btgn,bsgn->btsg', cc, bc)
        y_intra = jnp.einsum('btsg,btsgr,bsgr,bsgrp->btgrp', scores, decay, dtc, xc)
        y_state = jnp.einsum('btgn,bgrpn,btgr->btgrp', cc, state, jnp.exp(cum))
        last = cum[:, -1]
        w_end = jnp.exp(last[:, None] - cum) * dtc
        state = state * jnp.exp(last)[..., None, None] + jnp.einsum('bsgn,bsgr,bsgrp->bgrpn', bc, w_end, xc)
        return state, y_intra + y_state

    h0 = jnp.zeros((b, G, R, P, N), f32)
    _, y = lax.scan(step, h0, (xs, av, dts, bs, cs))
    return jnp.moveaxis(y, 0, 1).reshape(b, L, H, P)

def mamba2_bidir_mixer(h, w_in, conv_w, conv_b, dt_bias, a_log, d_skip, norm_g, w_out):
    bsz, L, _ = h.shape
    proj = h @ w_in
    z = proj[..., :D_INNER]
    xbc = proj[..., D_INNER:D_INNER + CONV_DIM]
    dt_raw = proj[..., D_INNER + CONV_DIM:]
    xbc = jax.nn.silu(dwconv_centred(xbc, conv_w) + conv_b.astype(xbc.dtype))
    xs = xbc[..., :D_INNER].reshape(bsz, L, N_SSM_HEADS, HEAD_DIM)
    bm = xbc[..., D_INNER:D_INNER + N_GROUPS * D_STATE].reshape(bsz, L, N_GROUPS, D_STATE)
    cm = xbc[..., D_INNER + N_GROUPS * D_STATE:].reshape(bsz, L, N_GROUPS, D_STATE)
    dt = jax.nn.softplus(dt_raw.astype(jnp.float32).reshape(bsz, L, 2, N_SSM_HEADS)
                         + dt_bias.astype(jnp.float32))
    a_neg = -jnp.exp(a_log.astype(jnp.float32))
    y_fwd = ssd_chunked(xs, dt[:, :, 0], a_neg[0], bm, cm)
    fl = lambda t: jnp.flip(t, axis=1)
    y_bwd = fl(ssd_chunked(fl(xs), fl(dt[:, :, 1]), a_neg[1], fl(bm), fl(cm)))
    y = y_fwd + y_bwd + d_skip.astype(jnp.float32)[:, None] * xs.astype(jnp.float32)
    u = (y.reshape(bsz, L, D_INNER) * jax.nn.silu(z.astype(jnp.float32))).reshape(bsz, L, N_GROUPS, D_INNER // N_GROUPS)
    u = u * lax.rsqrt(jnp.mean(u * u, axis=-1, keepdims=True) + EPS)
    u = u.reshape(bsz, L, D_INNER) * norm_g.astype(jnp.float32)
    return u.astype(h.dtype) @ w_out

def sq_relu_mlp(h, w1, w2):
    return jnp.square(jax.nn.relu(h @ w1)) @ w2

def setup_inputs(seed: int = 0) -> dict:
    key = jax.random.key(seed)
    ks = jax.random.split(key, 24)
    nrm = lambda k, shape, s: jax.random.normal(k, shape, jnp.float32) * s
    dt0 = jnp.exp(jax.random.uniform(ks[14], (N_SSD_LAYERS, 2, N_SSM_HEADS), jnp.float32)
                  * (np.log(0.1) - np.log(0.001)) + np.log(0.001))
    return {
        "x": nrm(ks[0], (BATCH, SEQ, D_MODEL), 1.0),
        "c": nrm(ks[1], (BATCH, D_MODEL), 1.0),
        "ada_w": nrm(ks[2], (DEPTH, 2, D_MODEL, 3 * D_MODEL), 0.5 * D_MODEL ** -0.5),
        "ada_b": nrm(ks[3], (DEPTH, 2, 3 * D_MODEL), 0.02),
        "norm_g": 1.0 + nrm(ks[4], (DEPTH, 2, D_MODEL), 0.1),
        "final_g": 1.0 + nrm(ks[5], (D_MODEL,), 0.1),
        "sc_in_w": nrm(ks[6], (N_SC_LAYERS, D_MODEL, 3 * D_MODEL), D_MODEL ** -0.5),
        "sc_conv_w": nrm(ks[7], (N_SC_LAYERS, D_MODEL, SC_CONV), SC_CONV ** -0.5),
        "sc_out_w": nrm(ks[8], (N_SC_LAYERS, D_MODEL, D_MODEL), D_MODEL ** -0.5),
        "m2_in_w": nrm(ks[9], (N_SSD_LAYERS, D_MODEL, IN_PROJ_DIM), D_MODEL ** -0.5),
        "m2_conv_w": nrm(ks[10], (N_SSD_LAYERS, CONV_DIM, SSM_CONV), SSM_CONV ** -0.5),
        "m2_conv_b": nrm(ks[11], (N_SSD_LAYERS, CONV_DIM), 0.02),
        "m2_dt_bias": dt0 + jnp.log(-jnp.expm1(-dt0)),
        "m2_a_log": jnp.log(jax.random.uniform(ks[12], (N_SSD_LAYERS, 2, N_SSM_HEADS), jnp.float32, 1.0, 16.0)),
        "m2_d": 1.0 + nrm(ks[13], (N_SSD_LAYERS, N_SSM_HEADS), 0.1),
        "m2_norm_g": 1.0 + nrm(ks[15], (N_SSD_LAYERS, D_INNER), 0.1),
        "m2_out_w": nrm(ks[16], (N_SSD_LAYERS, D_INNER, D_MODEL), D_INNER ** -0.5),
        "mlp_w1": nrm(ks[17], (DEPTH, D_MODEL, D_FF), D_MODEL ** -0.5),
        "mlp_w2": nrm(ks[18], (DEPTH, D_FF, D_MODEL), D_FF ** -0.5),
    }

def reference(x, c, ada_w, ada_b, norm_g, final_g, sc_in_w, sc_conv_w, sc_out_w,
              m2_in_w, m2_conv_w, m2_conv_b, m2_dt_bias, m2_a_log, m2_d, m2_norm_g, m2_out_w,
              mlp_w1, mlp_w2):
    cond = jax.nn.silu(c)

    def modulation(i, s):
        mod = cond @ ada_w[i, s] + ada_b[i, s]
        shift, scale, gate = jnp.split(mod, 3, axis=-1)
        return shift[:, None, :], scale[:, None, :], gate[:, None, :]

    for i in range(DEPTH):
        j = i // N_MIXERS
        shift, scale, gate = modulation(i, 0)
        h = rms_norm(x, norm_g[i, 0]) * (1.0 + scale) + shift
        if i % N_MIXERS == 0:
            out = short_conv_mixer(h, sc_in_w[j], sc_conv_w[j], sc_out_w[j])
        else:
            out = mamba2_bidir_mixer(h, m2_in_w[j], m2_conv_w[j], m2_conv_b[j], m2_dt_bias[j],
                                     m2_a_log[j], m2_d[j], m2_norm_g[j], m2_out_w[j])
        x = x + gate * out
        shift, scale, gate = modulation(i, 1)
        h = rms_norm(x, norm_g[i, 1]) * (1.0 + scale) + shift
        x = x + gate * sq_relu_mlp(h, mlp_w1[i], mlp_w2[i])
    return rms_norm(x, final_g)


_drawn_inputs = setup_inputs


def setup_inputs(seed=0):
    import zlib

    import numpy as np

    out = dict(_drawn_inputs(seed))
    spreads = {}
    factors = {'m2_conv_b': 8.0, 'm2_d': 4.932}
    for name, (base, spread) in spreads.items():
        noise = np.random.default_rng([zlib.crc32(name.encode()), seed]).standard_normal(out[name].shape)
        drawn = base * np.exp(spread * noise) if base else spread * noise
        out[name] = __import__('jax').numpy.asarray(drawn.astype(out[name].dtype))
    for name, factor in factors.items():
        out[name] = (out[name] * factor).astype(out[name].dtype)
    return out
```

```python
from contextlib import ExitStack

import numpy as np

import concourse.bass as bass
from concourse import mybir

P = 128
D = 2048
T = 256
KB = D // P
DI = 4096
HEADS = 64
HD = 64
NG = 8
N = 128
FF = 4 * D
EPS = 1e-6
HG = HEADS // NG
XB = DI // NG // P
HALF = KB // 2 * P

F32 = mybir.dt.float32
F32R = mybir.dt.float32r
BF16 = mybir.dt.bfloat16
ALU = mybir.AluOpType
ACT = mybir.ActivationFunctionType

U_CONV = 0
U_SCOUT = U_CONV + 3 * KB
U_MLP0 = U_SCOUT + KB
U_DT = U_MLP0 + 2 * FF // P
GU = 2 + 2 * XB
U_GA = U_DT + 1
GA = 5
U_OUT0 = U_GA + GA * GU
U_GB = U_OUT0 + KB
U_OUT1 = U_GB + (NG - GA) * GU
U_MLP1 = U_OUT1 + KB
UNITS = U_MLP1 + 2 * FF // P
ADA = 4 * 3 * KB
ADA_FIRST = 2 * KB
NEG = -1e30


DT_AV, DT_TOK, DT_CUM, DT_ALL = 10, 12, 13, 14


class At:

    def __init__(self, c, terms=()):
        self.c, self.terms = c, tuple(terms)

    def __add__(self, k):
        if isinstance(k, At):
            return At(self.c + k.c, self.terms + k.terms)
        return At(self.c + k, self.terms)

    def __sub__(self, k):
        return self + (-k)

    def __mul__(self, k):
        return At(self.c * k, [(r, a * k) for r, a in self.terms])

    def __floordiv__(self, k):
        assert all(a % k == 0 for _, a in self.terms)
        return At(self.c // k, [(r, a // k) for r, a in self.terms])

    def __mod__(self, k):
        assert all(a % k == 0 for _, a in self.terms)
        return self.c % k

    @property
    def v(self):
        out = self.c
        for r, a in self.terms:
            out = r * a + out
        return out


def at_least(e, sem, n):
    if isinstance(n, At):
        if not n.terms and n.c <= 0:
            return
        assert n.c >= 0, n.c
        n = n.v
    if isinstance(n, int) and n <= 0:
        return
    e.wait_ge(sem, n)


def first_unit(g):
    if not g.terms and g.c >= GA:
        return At(U_GB + (g.c - GA) * GU)
    return g * GU + U_GA


def blocks(g):
    return bass.ds((g * XB).v if g.terms else g.c * XB % KB, XB)


def loop(e, n, body):
    if n == 1:
        body(At(0))
    elif n > 1:
        with e.Fori(0, n) as i:
            body(At(0, [(i, 1)]))


def adas(n, ada_at, a):
    out, k = [], 0
    for s in range(n):
        out.append(a + k if s in ada_at else None)
        k += s in ada_at
    return out


def build(nc, w, ada, c, xT, adab, normg, scw, par, dtb, alog, out, cum_d):
    with ExitStack() as ctx:
        def sb(name, shape, dt=F32):
            return ctx.enter_context(nc.sbuf_tensor(name, shape, dt))

        def sem(name):
            return ctx.enter_context(nc.semaphore(name))

        x = sb("x", [P, KB, T])
        hcat = sb("hcat", [P, KB, 2 * T], F32R)
        hid = sb("hid", [P, KB, 2 * T], F32R)
        raw = sb("raw", [P, 4, HALF])
        wh = sb("wh", [P, 4, HALF], F32R)
        wl = sb("wl", [P, 4, HALF], F32R)
        adat = sb("adat", [P, 2, D])
        cond = sb("cond", [P, D])
        ta = sb("ta", [P, 2, T])
        tt = sb("tt", [P, 2, T])
        acc = sb("acc", [P, 2, T])
        th = sb("th", [P, 2, T])
        pad = sb("pad", [P, 2, T + 2])
        normt = sb("normt", [P, 6 * T])
        hv = normt[:, 0:4 * T].rearrange("p (k t) -> p k t", k=4)
        sq = normt[:, 4 * T:6 * T].rearrange("p (k t) -> p k t", k=2)
        ss = sb("ss", [P, T])
        rbc = sb("rbc", [P, T])
        modt = sb("modt", [P, 2])
        modc = sb("modc", [P, ADA])
        modb = sb("modb", [P, ADA])
        mods = sb("mods", [P, 4, 3, KB])
        ng_c = sb("ng_c", [P, 5, KB])
        scw_c = sb("scw_c", [P, KB, 3])
        parall = sb("parall", [P, NG, 32])
        parg = sb("parg", [P, 2, 32])
        dcol = sb("dcol", [P, 4])
        ones = sb("ones", [P, P])
        ident = sb("ident", [P, P])
        identr = sb("identr", [P, P], F32R)
        identb = sb("identb", [P, P], BF16)
        upf = sb("upf", [P, P])
        upb = sb("upb", [P, P])
        maskf = sb("maskf", [P, P], BF16)
        maskb = sb("maskb", [P, P], BF16)
        dtS = sb("dtS", [P, 2, 2, HEADS])
        ncS = sb("ncS", [P, 2, 2, HEADS])
        cumg = sb("cumg", [HG, 2, T])
        cgh = sb("cgh", [HG, 2, T], F32R)
        cgl = sb("cgl", [HG, 2, T], F32R)
        bT = sb("bT", [P, T])
        avS = bT[:, :].rearrange("p (c r) -> p c r", c=2)
        cT = sb("cT", [P, T])
        xs = sb("xs", [P, 2, XB, T])
        zs = sb("zs", [P, 2, XB, T])
        gf = sb("gf", [P, 3 * P])
        gb = sb("gb", [P, 3 * P])
        xd = sb("xd", [P, 2, 2, HG * HD])
        em = normt[:, :].rearrange("p (k t) -> p k t", k=4)
        ytok = xd[:, 0]
        dgrp = sb("dgrp", [P, 2, 2, HG])
        ngrp = sb("ngrp", [P, 2, 2, HG])

        psm = [ctx.enter_context(nc.psum_tensor(f"psm{i}", [P, 2 * T], F32)) for i in range(2)]
        psy = [ctx.enter_context(nc.psum_tensor(f"psy{i}", [P, 512], F32)) for i in range(2)]
        psr = [ctx.enter_context(nc.psum_tensor(f"psr{i}", [P, 512], F32)) for i in range(4)]

        raw_in = [sem(f"raw_in{i}") for i in range(4)]
        ada_in = [sem(f"ada_in{i}") for i in range(2)]
        small_in, x_in, c_in, out_done = sem("small_in"), sem("x_in"), sem("c_in"), sem("out_done")
        hi_done, lo_done, mm_done = sem("hi_done"), sem("lo_done"), sem("mm_done")
        copied, summed, stored = sem("copied"), sem("summed"), sem("stored")
        ada_done, mod_copied, mods_done, consts, silu_c = sem("ada_done"), sem("mod_copied"), sem("mods_done"), sem("consts"), sem("silu_c")
        pads, halved, idr = sem("pads"), sem("halved"), sem("idr")
        sq_done, ss_added, ss_zero, norm_sum = sem("sq_done"), sem("ss_added"), sem("ss_zero"), sem("norm_sum")
        rstd_a, rstd_b = sem("rstd_a"), sem("rstd_b")
        hv_done, hhi_done, hlo_done = sem("hv_done"), sem("hhi_done"), sem("hlo_done")
        sc_mid, sc_step, sc_conv, sc_gated, sc_hi = (sem(n) for n in ("sc_mid", "sc_step", "sc_conv", "sc_gated", "sc_hi"))
        relu_done, relu_hi = sem("relu_done"), sem("relu_hi")
        dt_act, dt_dve, dt_pe = sem("dt_act"), sem("dt_dve"), sem("dt_pe")
        cum_out, cum_in, cg_hi, cg_lo = sem("cum_out"), sem("cum_in"), sem("cg_hi"), sem("cg_lo")
        par_in, grp_in = sem("par_in"), sem("grp_in")
        mc_mid, mc_step, mc_conv, tanh_done = sem("mc_mid"), sem("mc_step"), sem("mc_conv"), sem("tanh_done")
        sg_scores, sg_xt, g_ready, xd_ready = sem("sg_scores"), sem("sg_xt"), sem("g_ready"), sem("xd_ready")
        cum_bc, exp_done, em_ready, y_head = sem("cum_bc"), sem("exp_done"), sem("em_ready"), sem("y_head")
        y_tok, y_back, v_done, vz_done, gsq = sem("y_tok"), sem("y_back"), sem("v_done"), sem("vz_done"), sem("gsq")
        gss, gsum, gr_a, gr_b, gu = sem("gss"), sem("gsum"), sem("gr_a"), sem("gr_b"), sem("gu")
        u_hi, u_lo = sem("u_hi"), sem("u_lo")
        fin, silu_mul = sem("fin"), sem("silu_mul")

        block = ctx.enter_context(nc.Block())

        def walk(e, conv, gated, relu, dt, group, scan, norm, gate=lambda n: None, lead=False):
            def bodies(n, f, peel=lead):
                if peel:
                    f(At(0), True)
                    if n > 1:
                        with e.Fori(0, n - 1) as i:
                            f(At(1, [(i, 1)]), False)
                else:
                    loop(e, n, lambda i: f(i, False))

            norm(0)
            bodies(KB // 2, lambda i, f: conv(i * 6 + U_CONV, i * 2, (0, 1, 3, 4), i * 4 + ADA_FIRST, f), True)
            a = ADA_FIRST + 4 * KB // 2
            gate(0)
            bodies(4, lambda i, f: gated(i * 4 + U_SCOUT, 0, i * 4, range(4), i * 4 + a, f, True, None))
            a += KB

            norm(1)
            bodies(4, lambda i, f: relu(i * 4 + U_MLP0, i * 4, i * 4, 1, range(4), i * 4 + a, f))
            a += KB
            gate(1)
            bodies(4, lambda i, f: gated(i * 4 + (U_MLP0 + KB), 1, i * 4, (), None, f, False, At(U_MLP0)))

            def quarter0(q, last):
                u = q * 32 + U_MLP0
                aq = q * 16 + (a - 16)
                loop(e, 4, lambda i: relu(u + i * 4, i * 4, q * 16 + i * 4, 1, (0, 2), aq + i * 2, False))
                bodies(4, lambda i, f: gated(u + i * 4 + KB, 1, i * 4, (0, 2), aq + i * 2 + 8, f, last, u))
            with e.Fori(0, 2) as q:
                quarter0(At(1, [(q, 1)]), False)
            quarter0(At(3), True)
            a += 48

            norm(2)
            dt()

            def g_unit(g):
                return first_unit(g), (1, 4, 7), g * 3 + a
            group(At(0), *g_unit(At(0)))
            with e.Fori(0, 2) as i:
                for k in (1, 2):
                    g = At(k, [(i, 2)])
                    group(g, *g_unit(g))
            gate(2)
            ao = a + 3 * GA
            bodies(4, lambda i, f: gated(i * 4 + U_OUT0, 2, i * 4, (0, 2), i * 2 + ao, f, False, "chunk 0"))
            a += 8
            for k in range(GA, NG):
                group(At(k), *g_unit(At(k)))
            scan(At(NG - 1))
            a += 3 * NG
            bodies(4, lambda i, f: gated(i * 4 + U_OUT1, 2, i * 4, (0, 2), i * 2 + a, f, True, "chunk 1"))
            a += 8

            norm(3)
            assert a + 8 == ADA
            for i in range(2):
                relu(At(i * 4 + U_MLP1), At(i * 4), At(i * 4 + 64), 3, range(4), At(i * 4 + a), lead and i == 0)
            loop(e, 2, lambda i: relu(i * 4 + (U_MLP1 + 8), i * 4 + 8, i * 4 + 72, 3, (), None, False))
            gate(3)
            bodies(4, lambda i, f: gated(i * 4 + (U_MLP1 + KB), 3, i * 4, (), None, f, False, At(U_MLP1)))
            with e.Fori(0, 2) as q:
                q = At(1, [(q, 1)])
                u = q * 32 + U_MLP1
                loop(e, 4, lambda i: relu(u + i * 4, i * 4, q * 16 + i * 4 + 64, 3, (), None, False))
                bodies(4, lambda i, f: gated(u + i * 4 + KB, 3, i * 4, (), None, f, False, u))
            u = At(U_MLP1 + 96)
            loop(e, 4, lambda i: relu(u + i * 4, i * 4, i * 4 + 112, 3, (), None, False))
            bodies(3, lambda i, f: gated(u + i * 4 + KB, 3, i * 4, (), None, f, True, u))
            gated(u + (KB + 12), 3, At(12), (), None, False, True, u)
            norm(4)

        @block.sync
        def _(sp):
            def load_half(h):
                if not h.terms and h.c >= 2 * UNITS:
                    return
                at_least(sp, lo_done, h - 3)
                sp.dma_start(raw[:, h % 4, :], w[h.v]).then_inc(raw_in[h % 4], 16)

            def load_ada(a):
                if not a.terms and a.c >= ADA:
                    return
                at_least(sp, ada_done, a - 1)
                sp.dma_start(adat[:, a % 2, :], ada[a.v]).then_inc(ada_in[a % 2], 16)

            sp.dma_start(cond[:, :], c.partition_broadcast(P)).then_inc(c_in, 16)
            load_ada(At(0))
            load_ada(At(1))
            for src, dst in ((adab, modb[:, :]), (normg, ng_c[:, :, :]), (scw, scw_c[:, :, :]),
                             (par, parall[:, :, :]), (dtb, dcol[:, 0:1]), (alog, dcol[:, 1:2])):
                sp.dma_start(dst, src).then_inc(small_in, 16)
            sp.dma_start(x[:, :, :], xT).then_inc(x_in, 16)
            for h in range(4):
                load_half(At(h))
            loop(sp, (ADA_FIRST - 2) // 2, lambda i: [load_ada(i * 2 + 2 + k) for k in range(2)])
            for h in range(4, 8):
                load_half(At(h))
            load_ada(At(ADA_FIRST))
            load_ada(At(ADA_FIRST + 1))

            def steps(u, n, ada_at, a):
                k = 0
                for s in range(n):
                    load_half((u + s) * 2 + 8)
                    load_half((u + s) * 2 + 9)
                    if s in ada_at:
                        load_ada(a + (k + 2))
                        k += 1

            def norm(n):
                if n < 4:
                    return
                for k in range(4):
                    at_least(sp, fin, 4 * (k + 1))
                    sp.dma_start(out[:, 4 * k:4 * k + 4, :], x[:, 4 * k:4 * k + 4, :]).then_inc(out_done, 16)
                sp.wait_ge(out_done, 64)

            walk(sp, lambda u, j, ada_at, a, f: steps(u, 6, ada_at, a),
                 lambda u, layer, n, ada_at, a, f, last, src: steps(u, 4, ada_at, a),
                 lambda u, j, r, layer, ada_at, a, f: steps(u, 4, ada_at, a),
                 lambda: steps(At(U_DT), 1, (), None),
                 lambda g, u, ada_at, a: steps(u, GU, ada_at, a),
                 lambda g: None, norm)

        @block.gpsimd
        def _(pool):
            pool.memset(ones[:, :], 1.0).then_inc(consts, 1)
            pool.memset(ident[:, :], 0.0).then_inc(consts, 1)
            pool.memset(maskf[:, :], 0.0).then_inc(consts, 1)
            pool.memset(maskb[:, :], 0.0).then_inc(consts, 1)
            pool.memset(ss[:, :], 0.0).then_inc(ss_zero, 1)
            pool.wait_ge(consts, 4)
            pool.affine_select(out=ident[:, :], in_=ident[:, :], compare_op=ALU.not_equal, fill=1.0, base=0,
                               pattern=[[-1, P]], channel_multiplier=1).then_inc(consts, 1)
            pool.affine_select(out=upf[:, :], in_=ones[:, :], compare_op=ALU.is_ge, fill=0.0, base=0,
                               pattern=[[1, P]], channel_multiplier=-1).then_inc(consts, 1)
            pool.affine_select(out=upb[:, :], in_=ones[:, :], compare_op=ALU.is_ge, fill=0.0, base=0,
                               pattern=[[-1, P]], channel_multiplier=1).then_inc(consts, 1)
            pool.affine_select(out=maskf[:, :], in_=maskf[:, :], compare_op=ALU.is_ge, fill=NEG, base=0,
                               pattern=[[1, P]], channel_multiplier=-1).then_inc(consts, 1)
            pool.affine_select(out=maskb[:, :], in_=maskb[:, :], compare_op=ALU.is_ge, fill=NEG, base=0,
                               pattern=[[-1, P]], channel_multiplier=1).then_inc(consts, 1)

            def keep(a):
                if a is not None:
                    at_least(pool, ada_done, a + 1)
                    pool.tensor_copy(modc[:, bass.ds(a.v, 1)], modt[:, a % 2:a % 2 + 1]).then_inc(mod_copied, 1)

            loop(pool, ADA_FIRST // 2, lambda i: [keep(i * 2 + k) for k in range(2)])

            def add_square(m):
                at_least(pool, sq_done, m + 1)
                at_least(pool, ss_added, m)
                pool.tensor_tensor(ss[:, :], ss[:, :], sq[:, m % 2, :], ALU.add).then_inc(ss_added, 1)

            def conv(u, j, ada_at, a, f):
                tiles = adas(6, ada_at, a)
                for k in range(2):
                    jj, v = j + k, u + 3 * k
                    at_least(pool, summed, v + 2)
                    pool.wait_ge(pads, 1)
                    pool.tensor_tensor(pad[:, k, 1:T + 1], tt[:, v % 2, :], tt[:, (v + 1) % 2, :],
                                       ALU.mult).then_inc(stored, 2)
                    at_least(pool, summed, v + 3)
                    at_least(pool, sc_conv, jj + 1)
                    pool.tensor_tensor(acc[:, k, :], tt[:, (v + 2) % 2, :], acc[:, k, :],
                                       ALU.mult).then_inc(sc_gated, 1)
                    at_least(pool, sc_hi, jj + 1)
                    pool.tensor_tensor(hid[:, jj.v, T:2 * T], acc[:, k, :], hid[:, jj.v, 0:T].bitcast(F32),
                                       ALU.subtract).then_inc(stored, 1)
                    for t in tiles[3 * k:3 * k + 3]:
                        keep(t)

            def gated(u, layer, n, ada_at, a, f, last, src):
                tiles = adas(4, ada_at, a)
                for s in range(4):
                    v, nn = u + s, n + s
                    at_least(pool, summed, v + 1)
                    at_least(pool, stored, v)
                    pool.tensor_tensor(x[:, nn.v, :], x[:, nn.v, :], tt[:, v % 2, :], ALU.add).then_inc(stored, 1)
                    keep(tiles[s])
                    if last:
                        add_square(nn + (layer + 1) * KB)

            def relu(u, j, r, layer, ada_at, a, f):
                tiles = adas(4, ada_at, a)
                for s in range(4):
                    v, jj = u + s, j + s
                    at_least(pool, relu_hi, r + (s + 1))
                    pool.tensor_tensor(hid[:, jj.v, T:2 * T], tt[:, v % 2, :], hid[:, jj.v, 0:T].bitcast(F32),
                                       ALU.subtract).then_inc(stored, 1)
                    keep(tiles[s])

            def dt():
                pool.wait_ge(dt_dve, DT_CUM)
                pool.dma_start(cum_d.rearrange("d g h t -> (d g h) t"), hv[:, 0, :]).then_inc(cum_out, 16)

            def unit_store(g, v, s):
                at_least(pool, tanh_done, g * GU + (s + 1))
                at_least(pool, stored, v)
                par2 = g % 2
                if s < 2:
                    at_least(pool, sg_scores, g)
                    src, dst = acc[:, v % 2, :], (bT, cT)[s][:, :]
                else:
                    at_least(pool, u_lo, g - 1)
                    if s < 2 + XB:
                        src, dst = acc[:, v % 2, :], xs[:, par2, s - 2, :]
                    else:
                        src, dst = tt[:, v % 2, :], zs[:, par2, s - 2 - XB, :]
                t = th[:, v % 2, :]
                pool.tensor_tensor(t, t, src, ALU.mult).then_inc(silu_mul, 1)
                at_least(pool, silu_mul, g * GU + (s + 1))
                pool.tensor_tensor(dst, t, src, ALU.add).then_inc(stored, 1)

            def scan_piece(g, s):
                par2 = g % 2
                flat = lambda b, lo, hi: b[:, par2, lo:hi, :].rearrange("p b t -> p (b t)")
                if s == 7:
                    at_least(pool, v_done, g * XB + XB)
                    at_least(pool, stored, first_unit(g) + GU)
                    pool.tensor_tensor(flat(xs, 0, XB), flat(xs, 0, XB), flat(zs, 0, XB), ALU.mult)\
                        .then_inc(vz_done, 1)
                    at_least(pool, gsq, g + 1)
                    pool.tensor_tensor(flat(zs, 0, 2), flat(zs, 0, 2), flat(zs, 2, 4), ALU.add).then_inc(gss, 1)
                    at_least(pool, gss, g * 2 + 1)
                    pool.tensor_tensor(flat(zs, 0, 1), flat(zs, 0, 1), flat(zs, 1, 2), ALU.add).then_inc(gss, 1)
                if s == 9:
                    at_least(pool, u_hi, g + 1)
                    pool.tensor_tensor(hid[:, blocks(g), T:2 * T], xs[:, par2, :, :],
                                       hid[:, blocks(g), 0:T].bitcast(F32), ALU.subtract).then_inc(u_lo, 1)

            def group(g, u, ada_at, a):
                at_least(pool, gu, g * XB - XB)
                pool.wait_ge(halved, 1)
                pool.tensor_copy(parg[:, g % 2, :], parall[:, g.v, :]).then_inc(par_in, 1)
                tiles = adas(GU, ada_at, a)
                for s in range(GU):
                    if g.terms or g.c:
                        scan_piece(g - 1, s)
                    unit_store(g, u + s, s)
                    keep(tiles[s])
                    if s == 5:
                        at_least(pool, cg_lo, g)
                        pool.wait_ge(cum_out, 16)
                        pool.dma_start(cumg[:, :, :], cum_d.rearrange("d g h t -> g h d t")[g.v])\
                            .then_inc(cum_in, 16)

            def scan(g):
                for s in range(10):
                    scan_piece(g, s)

            def norm(n):
                if n == 0:
                    for m in range(KB):
                        if m == 0:
                            pool.wait_ge(ss_zero, 1)
                        add_square(At(m))
                at_least(pool, norm_sum, n + 1)
                pool.memset(ss[:, :], 0.0).then_inc(ss_zero, 1)
                at_least(pool, ss_zero, n + 2)

            walk(pool, conv, gated, relu, dt, group, scan, norm)

        @block.scalar
        def _(act):
            def hi(h):
                if not h.terms and h.c >= 2 * UNITS:
                    return
                at_least(act, raw_in[h % 4], (h - h % 4) * 4 + 16)
                at_least(act, mm_done, h - 3)
                act.activation(wh[:, h % 4, :], raw[:, h % 4, :], ACT.Copy).then_inc(hi_done, 1)

            def copy(v, scale=1.0):
                at_least(act, mm_done, v * 2 + 2)
                at_least(act, summed, v - 1)
                act.activation(ta[:, v % 2, :], psm[v % 2][:, 0:T], ACT.Copy, scale=scale).then_inc(copied, 1)

            def square(m, src):
                at_least(act, ss_added, m - 1)
                act.activation(sq[:, m % 2, :], src, ACT.Square).then_inc(sq_done, 1)

            def step(v, scale=1.0):
                hi(v * 2 + 4)
                copy(v, scale)
                hi(v * 2 + 5)

            act.wait_ge(c_in, 16)
            act.activation(cond[:, :], cond[:, :], ACT.Silu).then_inc(silu_c, 1)
            for h in range(4):
                hi(At(h))

            def conv(u, j, ada_at, a, f):
                for k in range(2):
                    jj, v = j + k, u + 3 * k
                    step(v)
                    step(v + 1)
                    at_least(act, stored, v + 2)
                    act.activation(acc[:, k, :], pad[:, k, 1:T + 1], ACT.Copy,
                                   scale=scw_c[:, jj.v, 1:2]).then_inc(sc_mid, 1)
                    step(v + 2)
                    at_least(act, sc_gated, jj + 1)
                    act.activation(hid[:, jj.v, 0:T], acc[:, k, :], ACT.Copy).then_inc(sc_hi, 1)

            def gated(u, layer, n, ada_at, a, f, last, src):
                at_least(act, mods_done, 4 * layer + 4)
                for s in range(4):
                    v, nn = u + s, n + s
                    step(v, mods[:, layer, 2, bass.ds(nn.v, 1)])
                    if last:
                        at_least(act, stored, v + 1)
                        square(nn + (layer + 1) * KB, x[:, nn.v, :])

            def relu(u, j, r, layer, ada_at, a, f):
                for s in range(4):
                    v, jj = u + s, j + s
                    step(v)
                    at_least(act, relu_done, r + (s + 1))
                    act.activation(hid[:, jj.v, 0:T], tt[:, v % 2, :], ACT.Copy).then_inc(relu_hi, 1)

            def dt():
                v = At(U_DT)
                step(v)
                at_least(act, summed, v + 1)
                act.activation(th[:, 0, :], tt[:, v % 2, :], ACT.Abs, bias=dcol[:, 0:1]).then_inc(dt_act, 1)
                act.wait_ge(dt_act, 1)
                act.activation(th[:, 0, :], th[:, 0, :], ACT.Exp, scale=-1.0).then_inc(dt_act, 1)
                act.activation(dcol[:, 2:3], dcol[:, 1:2], ACT.Exp).then_inc(dt_act, 1)
                act.wait_ge(dt_dve, 1)
                act.activation(hv[:, 0, :], hv[:, 1, :], ACT.Ln).then_inc(dt_act, 1)

            def unit(g, v, s):
                conv_unit = s < 2 + XB
                hi(v * 2 + 4)
                copy(v, 1.0 if conv_unit else 0.5)
                hi(v * 2 + 5)
                par2 = g % 2
                if conv_unit:
                    at_least(act, summed, v + 1)
                    at_least(act, par_in, g + 1)
                    at_least(act, stored, v - 1)
                    act.activation(acc[:, v % 2, :], pad[:, v % 2, 1:T + 1], ACT.Identity,
                                   bias=parg[:, par2, 18 + s:19 + s],
                                   scale=parg[:, par2, 3 * s + 1:3 * s + 2]).then_inc(mc_mid, 1)
                    at_least(act, mc_conv, g * 6 + (s + 1))
                    act.activation(th[:, v % 2, :], acc[:, v % 2, :], ACT.Tanh).then_inc(tanh_done, 1)
                else:
                    at_least(act, summed, v + 1)
                    at_least(act, stored, v - 1)
                    act.activation(th[:, v % 2, :], tt[:, v % 2, :], ACT.Tanh).then_inc(tanh_done, 1)

            def scan_piece(g, s):
                par2 = g % 2
                if s == 0:
                    at_least(act, cum_in, g * 16 + 16)
                    at_least(act, y_head, g * HG)
                    act.activation(cgh[:, :, :], cumg[:, :, :], ACT.Copy).then_inc(cg_hi, 1)
                if 1 <= s <= 4:
                    at_least(act, grp_in, g * 2 + 2)
                    for k in range(4):
                        h, d = 2 * (s - 1) + k // 2, k % 2
                        first, second = (0, 1) if d == 0 else (1, 0)
                        at_least(act, cum_bc, g * 16 + (4 * (s - 1) + k + 1))
                        at_least(act, y_head, g * HG + max(h - 1, 0))
                        act.activation(em[:, k, 0:T], psr[k][:, 0:T], ACT.Exp,
                                       bias=ngrp[:, first, d, h:h + 1])
                        act.activation(em[:, k, T:3 * P], psr[k][:, T:3 * P], ACT.Exp,
                                       bias=ngrp[:, second, d, h:h + 1]).then_inc(exp_done, 1)
                if s == 5:
                    at_least(act, y_head, g * HG + HG)
                    for ch in range(2):
                        act.activation(ytok[:, ch, :], psy[ch][:, :], ACT.Copy).then_inc(y_tok, 1)
                if s == 7:
                    at_least(act, vz_done, g + 1)
                    act.activation(zs[:, par2, :, :], xs[:, par2, :, :], ACT.Square).then_inc(gsq, 1)
                if s == 8:
                    at_least(act, gr_a, g * 2 + 2)
                    act.activation(rbc[:, :], rbc[:, :], ACT.Sqrt).then_inc(gr_b, 1)
                if s == 9:
                    at_least(act, gu, g * XB + XB)
                    act.activation(hid[:, blocks(g), 0:T], xs[:, par2, :, :], ACT.Copy).then_inc(u_hi, 1)

            def group(g, u, ada_at, a):
                for s in range(GU):
                    if g.terms or g.c:
                        scan_piece(g - 1, s)
                    unit(g, u + s, s)

            def scan(g):
                for s in range(10):
                    scan_piece(g, s)

            def norm(n):
                if n == 0:
                    act.wait_ge(x_in, 16)
                    for m in range(KB):
                        square(At(m), x[:, m, :])
                at_least(act, rstd_a, 2 * n + 2)
                act.activation(rbc[:, :], rbc[:, :], ACT.Sqrt).then_inc(rstd_b, 1)
                if n == 4:
                    return
                at_least(act, mods_done, 4 * n + 3)
                for k in range(KB):
                    at_least(act, hv_done, n * KB + k + 1)
                    act.activation(hcat[:, k, 0:T], hv[:, k % 4, :], ACT.Identity,
                                   bias=mods[:, n, 0, k:k + 1]).then_inc(hhi_done, 1)

            walk(act, conv, gated, relu, dt, group, scan, norm)

        @block.tensor
        def _(pe):
            def unit(u, src, ready=None):
                bank = psm[u % 2]
                for half in range(2):
                    h = u * 2 + half
                    at_least(pe, lo_done, h + 1)
                    if half == 0:
                        at_least(pe, summed, u - 1)
                    for k in range(KB // 2):
                        kb = half * KB // 2 + k
                        if ready:
                            ready(kb)
                        pe.matmul(bank[:, :], wh[:, h % 4, k * P:(k + 1) * P], src[:, kb, :],
                                  start=(kb == 0), stop=(kb == KB - 1), skip_group_check=True)
                        mm = pe.matmul(bank[:, T:2 * T], wl[:, h % 4, k * P:(k + 1) * P], src[:, kb, 0:T],
                                       start=False, stop=(kb == KB - 1), skip_group_check=True)
                    mm.then_inc(mm_done, 1)

            def norm_ready(n):
                return lambda kb: at_least(pe, hlo_done, n * KB + kb + 1)

            def conv(u, j, ada_at, a, first):
                for s in range(6):
                    unit(u + s, hcat, norm_ready(0) if first and s == 0 else None)

            def gated(u, layer, n, ada_at, a, first, last, src):
                def ready(kb):
                    if src in ("chunk 0", "chunk 1"):
                        if kb % XB == 0:
                            at_least(pe, u_lo, kb // XB + (1 if src == "chunk 0" else 1 + NG // 2))
                    elif isinstance(src, At):
                        at_least(pe, stored, src + (kb + 1))
                    else:
                        at_least(pe, stored, 3 * (kb + 1))
                for s in range(4):
                    unit(u + s, hid, ready if first and s == 0 else None)

            def relu(u, j, r, layer, ada_at, a, first):
                for s in range(4):
                    unit(u + s, hcat, norm_ready(layer) if first and s == 0 else None)

            def dt():
                unit(At(U_DT), hcat, norm_ready(2))
                pe.wait_ge(consts, 9)
                pe.wait_ge(dt_dve, DT_AV)
                for i, src in ((0, acc[:, 0, :]), (1, acc[:, 1, :])):
                    for ch in range(2):
                        mm = pe.transpose(psr[i][:, ch * P:(ch + 1) * P], src[:, ch * P:(ch + 1) * P], ident[:, :])
                mm.then_inc(dt_pe, 1)
                pe.wait_ge(dt_dve, DT_TOK)
                f, b = slice(0, HEADS), slice(HEADS, P)
                for rows, up, near, far in ((f, upf, 0, 1), (b, upb, 1, 0)):
                    pe.matmul(psr[2][rows, near * P:(near + 1) * P], avS[:, near, rows], up[:, :],
                              start=True, stop=True, skip_group_check=True)
                    pe.matmul(psr[2][rows, far * P:(far + 1) * P], avS[:, near, rows], ones[:, :],
                              start=False, stop=False, skip_group_check=True)
                    mm = pe.matmul(psr[2][rows, far * P:(far + 1) * P], avS[:, far, rows], up[:, :],
                                   start=False, stop=True, skip_group_check=True)
                mm.then_inc(dt_pe, 1)
                pe.wait_ge(dt_dve, DT_CUM)
                for ch in range(2):
                    mm = pe.transpose(psr[3][:, ch * P:(ch + 1) * P], hv[:, 0, ch * P:(ch + 1) * P], ident[:, :])
                mm.then_inc(dt_pe, 1)

            def scan_piece(g, s):
                par2 = g % 2
                if s == 0:
                    at_least(pe, stored, first_unit(g) + 2 + XB)
                    at_least(pe, v_done, g * XB)
                    at_least(pe, gr_a, g * 2)
                    at_least(pe, dt_dve, DT_ALL)
                    for ch in range(2):
                        mm = pe.matmul(psr[0][:, ch * T:(ch + 1) * T], bT[:, ch * P:(ch + 1) * P], cT[:, :],
                                       start=True, stop=True, skip_group_check=True)
                    mm.then_inc(sg_scores, 1)
                    at_least(pe, y_tok, g * 2)
                    for ch in range(2):
                        for b in range(XB):
                            mm = pe.transpose(psy[ch][:, b * P:(b + 1) * P], xs[:, par2, b, ch * P:(ch + 1) * P],
                                              ident[:, :])
                    mm.then_inc(sg_xt, 1)
                if 2 <= s <= 5:
                    for h in (2 * (s - 2), 2 * (s - 2) + 1):
                        if h == 0:
                            at_least(pe, xd_ready, g * 4 + 4)
                        at_least(pe, em_ready, g * 16 + (2 * h + 2))
                        mf, mb = em[:, 2 * (h % 2), :], em[:, 2 * (h % 2) + 1, :]
                        cols = slice(h * HD, (h + 1) * HD)
                        for ch, terms in ((0, ((mf, 0, 0, 0), (mb, 2 * P, 1, 0), (mb, 0, 1, 1))),
                                          (1, ((mf, P, 0, 0), (mf, 2 * P, 0, 1), (mb, P, 1, 1)))):
                            for i, (m, at, d, sc) in enumerate(terms):
                                mm = pe.matmul(psy[ch][:, cols], m[:, at:at + P], xd[:, d, sc, cols],
                                               start=(i == 0), stop=(i == 2), skip_group_check=True)
                        mm.then_inc(y_head, 1)
                if 1 <= s <= 4:
                    if s == 1:
                        at_least(pe, cg_lo, g + 1)
                        at_least(pe, g_ready, g * 4 + 4)
                    for k in range(4):
                        h, d = 2 * (s - 1) + k // 2, k % 2
                        at_least(pe, exp_done, g * 16 + max(4 * (s - 1) + k - 3, 0))
                        one = identr[0:HG, h:h + 1].to_broadcast([HG, P])
                        far = slice(P, T) if d == 0 else slice(0, P)
                        for i, cg in enumerate((cgh, cgl)):
                            pe.matmul(psr[k][:, 0:T], one, cg[:, d, :], start=(i == 0), stop=False,
                                      skip_group_check=True)
                            pe.matmul(psr[k][:, T:3 * P], one, cg[:, d, far], start=False, stop=False,
                                      skip_group_check=True)
                        mask, near = (maskf, 0) if d == 0 else (maskb, P)
                        pe.matmul(psr[k][:, near:near + P], identb[:, :], mask[:, :], start=False, stop=False,
                                  skip_group_check=True)
                        pe.matmul(psr[k][:, T:3 * P], identb[:, :], mask[:, :], start=False, stop=True,
                                  skip_group_check=True).then_inc(cum_bc, 1)
                if s == 6:
                    at_least(pe, y_tok, g * 2 + 2)
                    at_least(pe, exp_done, g * 16 + 16)
                    for b in range(XB):
                        for ch in range(2):
                            at = (b % 2) * T + ch * P
                            mm = pe.transpose(psr[b // 2][:, at:at + P], ytok[:, ch, b * P:(b + 1) * P],
                                              ident[:, :])
                    mm.then_inc(y_back, 1)
                if s == 8:
                    at_least(pe, gss, g * 2 + 2)
                    pe.matmul(psr[2][:, 0:T], ones[:, :], zs[:, par2, 0, :], start=True, stop=True,
                              skip_group_check=True).then_inc(gsum, 1)

            def group(g, u, ada_at, a):
                for s in range(GU):
                    if g.terms or g.c:
                        scan_piece(g - 1, s)
                    unit(u + s, hcat)

            def scan(g):
                for s in range(10):
                    scan_piece(g, s)

            def norm(n):
                if n == 0:
                    pe.wait_ge(consts, 9)
                    pe.wait_ge(idr, 2)
                at_least(pe, ss_added, KB * (n + 1))
                if n == 3:
                    at_least(pe, gr_a, 2 * NG)
                pe.matmul(psr[2][:, 0:T], ones[:, :], ss[:, :], start=True, stop=True,
                          skip_group_check=True).then_inc(norm_sum, 1)

            walk(pe, conv, gated, relu, dt, group, scan, norm, lead=True)

        @block.vector
        def _(dve):
            def lo(h):
                if not h.terms and h.c >= 2 * UNITS:
                    return
                at_least(dve, hi_done, h + 1)
                dve.tensor_tensor(wl[:, h % 4, :], raw[:, h % 4, :], wh[:, h % 4, :].bitcast(F32),
                                  ALU.subtract).then_inc(lo_done, 1)

            def tile(a):
                at_least(dve, ada_in[a % 2], (a - a % 2) * 8 + 16)
                t = adat[:, a % 2, :]
                at_least(dve, mod_copied, a - 1)
                dve.tensor_tensor_reduce(t, t, cond[:, :], 1.0, 0.0, ALU.mult, ALU.add,
                                         modt[:, a % 2:a % 2 + 1]).then_inc(ada_done, 1)

            def step(v, add, rest=None, ada=None):
                lo(v * 2 + 4)
                at_least(dve, copied, v + 1)
                add(v).then_inc(summed, 1)
                lo(v * 2 + 5)
                if rest:
                    rest()
                if ada is not None:
                    tile(ada)

            def add_tt(v):
                at_least(dve, stored, v - 1)
                return dve.tensor_tensor(tt[:, v % 2, :], ta[:, v % 2, :], psm[v % 2][:, T:2 * T], ALU.add)

            def modulation(n, which):
                at_least(dve, mod_copied, 3 * KB * n + KB * (which + 1))
                cols = slice(3 * KB * n + KB * which, 3 * KB * n + KB * (which + 1))
                dve.tensor_tensor(mods[:, n, which, :], modc[:, cols], modb[:, cols], ALU.add).then_inc(mods_done, 1)
                if which == 1:
                    at_least(dve, mods_done, 4 * n + 2)
                    dve.scalar_tensor_tensor(out=mods[:, n, 1, :], in0=mods[:, n, 1, :], scalar=1.0,
                                             in1=ng_c[:, n, :], op0=ALU.add, op1=ALU.mult).then_inc(mods_done, 1)

            dve.memset(pad[:, :, :], 0.0).then_inc(pads, 1)
            dve.wait_ge(consts, 9)
            dve.tensor_copy(identr[:, :], ident[:, :]).then_inc(idr, 1)
            dve.tensor_copy(identb[:, :], ident[:, :]).then_inc(idr, 1)
            dve.wait_ge(small_in, 96)
            dve.tensor_scalar(parall[:, :, 0:24], parall[:, :, 0:24], 0.5, None, ALU.mult).then_inc(halved, 1)
            dve.wait_ge(silu_c, 1)
            tile(At(0))
            tile(At(1))
            loop(dve, (ADA_FIRST - 2) // 2, lambda i: [tile(i * 2 + 2 + k) for k in range(2)])
            for h in range(4):
                lo(At(h))

            def conv(u, j, ada_at, a, f):
                tiles = adas(6, ada_at, a)
                for k in range(2):
                    jj, v = j + k, u + 3 * k
                    step(v, add_tt, None, tiles[3 * k])
                    step(v + 1, add_tt, None, tiles[3 * k + 1])

                    def taps():
                        at_least(dve, sc_mid, jj + 1)
                        dve.scalar_tensor_tensor(out=acc[:, k, :], in0=pad[:, k, 0:T], scalar=scw_c[:, jj.v, 0:1],
                                                 in1=acc[:, k, :], op0=ALU.mult, op1=ALU.add).then_inc(sc_step, 1)
                        at_least(dve, sc_step, jj + 1)
                        dve.scalar_tensor_tensor(out=acc[:, k, :], in0=pad[:, k, 2:T + 2],
                                                 scalar=scw_c[:, jj.v, 2:3], in1=acc[:, k, :], op0=ALU.mult,
                                                 op1=ALU.add).then_inc(sc_conv, 1)
                    step(v + 2, add_tt, taps, tiles[3 * k + 2])

            def gate(layer):
                modulation(layer, 2)

            def gated(u, layer, n, ada_at, a, f, last, src):
                tiles = adas(4, ada_at, a)

                for s in range(4):
                    nn = n + s
                    gcol = mods[:, layer, 2, bass.ds(nn.v, 1)]

                    def add(v):
                        at_least(dve, stored, v - 1)
                        return dve.scalar_tensor_tensor(out=tt[:, v % 2, :], in0=psm[v % 2][:, T:2 * T], scalar=gcol,
                                                        in1=ta[:, v % 2, :], op0=ALU.mult, op1=ALU.add)
                    step(u + s, add, None, tiles[s])

            def relu(u, j, r, layer, ada_at, a, f):
                tiles = adas(4, ada_at, a)
                for s in range(4):
                    v = u + s

                    def square():
                        at_least(dve, summed, v + 1)
                        t = tt[:, v % 2, :]
                        dve.scalar_tensor_tensor(out=t, in0=t, scalar=0.0, in1=t, op0=ALU.max,
                                                 op1=ALU.mult).then_inc(relu_done, 1)
                    step(v, add_tt, square, tiles[s])

            def dt():
                v = At(U_DT)
                step(v, add_tt)
                n = [0]

                def own(ins):
                    n[0] += 1
                    ins.then_inc(dt_dve, 1)

                e, e1, m, r = th[:, 0, :], hv[:, 1, :], hv[:, 2, :], hv[:, 3, :]
                dve.wait_ge(dt_act, 2)
                own(dve.tensor_scalar(e1, e, 1.0, None, ALU.add))
                dve.wait_ge(dt_dve, 1)
                own(dve.tensor_scalar(r, e1, -1.0, None, ALU.add))
                dve.wait_ge(dt_dve, 2)
                own(dve.tensor_scalar(m, r, 0.0, None, ALU.is_equal))
                dve.wait_ge(dt_dve, 3)
                own(dve.tensor_tensor(r, r, m, ALU.add))
                dve.wait_ge(dt_dve, 4)
                own(dve.reciprocal(r, r))
                dve.wait_ge(dt_dve, 5)
                own(dve.tensor_tensor(r, r, e, ALU.mult))
                dve.wait_ge(dt_act, 4)
                own(dve.tensor_tensor(m, m, hv[:, 0, :], ALU.add))
                dve.wait_ge(dt_dve, 7)
                own(dve.tensor_tensor(r, r, m, ALU.mult))
                own(dve.tensor_scalar(acc[:, 0, :], tt[:, v % 2, :], dcol[:, 0:1], 0.0, ALU.add, ALU.max))
                dve.wait_ge(dt_dve, 9)
                at_least(dve, stored, v)
                dve.tensor_tensor(acc[:, 0, :], acc[:, 0, :], r, ALU.add).then_inc(stored, 1)
                at_least(dve, stored, v + 1)
                own(dve.tensor_scalar(acc[:, 1, :], acc[:, 0, :], dcol[:, 2:3], -1.0, ALU.mult, ALU.mult))
                assert n[0] == DT_AV
                dve.wait_ge(dt_pe, 1)
                own(dve.tensor_copy(dtS[:, :, :, :].rearrange("p c d h -> p (c d h)"), psr[0][:, 0:T]))
                own(dve.tensor_copy(avS[:, :, :].rearrange("p c r -> p (c r)"), psr[1][:, 0:T]))
                assert n[0] == DT_TOK
                dve.wait_ge(dt_pe, 2)
                own(dve.tensor_copy(hv[:, 0, :], psr[2][:, 0:T]))
                assert n[0] == DT_CUM
                dve.wait_ge(dt_pe, 3)
                own(dve.tensor_scalar(ncS[:, :, :, :].rearrange("p c d h -> p (c d h)"), psr[3][:, 0:T], -1.0, None,
                                      ALU.mult))
                assert n[0] == DT_ALL

            def unit(g, v, s, ada):
                par2 = g % 2
                if s < 2 + XB:
                    def add(v):
                        at_least(dve, mc_conv, g * 6 + (s - 1))
                        return dve.tensor_tensor(pad[:, v % 2, 1:T + 1], ta[:, v % 2, :], psm[v % 2][:, T:2 * T],
                                                 ALU.add)

                    def taps():
                        a = acc[:, v % 2, :]
                        at_least(dve, mc_mid, g * 6 + (s + 1))
                        dve.scalar_tensor_tensor(out=a, in0=pad[:, v % 2, 0:T], scalar=parg[:, par2, 3 * s:3 * s + 1],
                                                 in1=a, op0=ALU.mult, op1=ALU.add).then_inc(mc_step, 1)
                        at_least(dve, mc_step, g * 6 + (s + 1))
                        dve.scalar_tensor_tensor(out=a, in0=pad[:, v % 2, 2:T + 2],
                                                 scalar=parg[:, par2, 3 * s + 2:3 * s + 3], in1=a, op0=ALU.mult,
                                                 op1=ALU.add).then_inc(mc_conv, 1)
                    step(v, add, taps, ada)
                else:
                    def add(v):
                        at_least(dve, stored, v - 1)
                        return dve.scalar_tensor_tensor(out=tt[:, v % 2, :], in0=psm[v % 2][:, T:2 * T], scalar=0.5,
                                                        in1=ta[:, v % 2, :], op0=ALU.mult, op1=ALU.add)
                    step(v, add, None, ada)

            def scan_piece(g, s):
                par2 = g % 2
                if s == 0:
                    at_least(dve, exp_done, g * 16)
                    at_least(dve, dt_dve, DT_ALL)
                    for dst, src in ((ngrp, ncS), (dgrp, dtS)):
                        cols = src[:, :, :, :].rearrange("p c d (g h) -> p c d g h", g=NG)
                        dve.tensor_copy(dst[:, :, :, :], cols[:, :, :, g.v, :]).then_inc(grp_in, 1)
                    at_least(dve, cg_hi, g + 1)
                    dve.tensor_tensor(cgl[:, :, :], cumg[:, :, :], cgh[:, :, :].bitcast(F32), ALU.subtract)\
                        .then_inc(cg_lo, 1)
                    at_least(dve, sg_scores, g + 1)
                    for dst, at, lo_, hi_ in ((gf, 0, 0, T), (gf, T, T + P, 2 * T), (gb, 0, T, 2 * T), (gb, T, 0, P)):
                        dve.tensor_copy(dst[:, at:at + hi_ - lo_], psr[0][:, lo_:hi_]).then_inc(g_ready, 1)
                    at_least(dve, sg_xt, g + 1)
                    at_least(dve, grp_in, g * 2 + 2)
                    at_least(dve, y_back, g)
                    for d in range(2):
                        for ch in range(2):
                            dve.tensor_tensor(
                                xd[:, d, ch, :].rearrange("p (h e) -> p h e", e=HD),
                                psy[ch][:, :].rearrange("p (h e) -> p h e", e=HD),
                                dgrp[:, ch, d, :].unsqueeze(2).to_broadcast([P, HG, HD]),
                                ALU.mult).then_inc(xd_ready, 1)
                if 1 <= s <= 4:
                    if s == 1:
                        at_least(dve, g_ready, g * 4 + 4)
                    for k in range(4):
                        at_least(dve, exp_done, g * 16 + (4 * (s - 1) + k + 1))
                        dve.tensor_tensor(em[:, k, :], em[:, k, :], (gf, gb)[k % 2][:, :], ALU.mult)\
                            .then_inc(em_ready, 1)
                if s == 6:
                    at_least(dve, y_back, g + 1)
                    for b in range(XB):
                        v = xs[:, par2, b, :]
                        dve.scalar_tensor_tensor(out=v, in0=v, scalar=parg[:, par2, 28 + b:29 + b],
                                                 in1=psr[b // 2][:, (b % 2) * T:(b % 2) * T + T],
                                                 op0=ALU.mult, op1=ALU.add).then_inc(v_done, 1)
                if s == 8:
                    at_least(dve, gsum, g + 1)
                    dve.tensor_scalar(rbc[:, :], psr[2][:, 0:T], 1.0 / (XB * P), EPS, ALU.mult, ALU.add)\
                        .then_inc(gr_a, 1)
                    at_least(dve, gr_a, g * 2 + 1)
                    dve.reciprocal(rbc[:, :], rbc[:, :]).then_inc(gr_a, 1)
                    at_least(dve, gr_b, g + 1)
                    for b in range(XB):
                        v = xs[:, par2, b, :]
                        dve.scalar_tensor_tensor(out=v, in0=v, scalar=parg[:, par2, 24 + b:25 + b], in1=rbc[:, :],
                                                 op0=ALU.mult, op1=ALU.mult).then_inc(gu, 1)

            def group(g, u, ada_at, a):
                tiles = adas(GU, ada_at, a)
                for s in range(GU):
                    if g.terms or g.c:
                        scan_piece(g - 1, s)
                    unit(g, u + s, s, tiles[s])

            def scan(g):
                for s in range(10):
                    scan_piece(g, s)

            def norm(n):
                if n < 4:
                    modulation(n, 0)
                    modulation(n, 1)
                at_least(dve, norm_sum, n + 1)
                dve.tensor_scalar(rbc[:, :], psr[2][:, 0:T], 1.0 / D, EPS, ALU.mult, ALU.add).then_inc(rstd_a, 1)
                at_least(dve, rstd_a, 2 * n + 1)
                dve.reciprocal(rbc[:, :], rbc[:, :]).then_inc(rstd_a, 1)
                at_least(dve, rstd_b, n + 1)
                if n == 4:
                    for k in range(KB):
                        dve.scalar_tensor_tensor(out=x[:, k, :], in0=x[:, k, :], scalar=ng_c[:, 4, k:k + 1],
                                                 in1=rbc[:, :], op0=ALU.mult, op1=ALU.mult).then_inc(fin, 1)
                    return
                at_least(dve, mods_done, 4 * n + 3)
                for k in range(KB + 2):
                    if k < KB:
                        if k >= 4:
                            at_least(dve, hlo_done, n * KB + k - 3)
                        dve.scalar_tensor_tensor(out=hv[:, k % 4, :], in0=x[:, k, :], scalar=mods[:, n, 1, k:k + 1],
                                                 in1=rbc[:, :], op0=ALU.mult, op1=ALU.mult).then_inc(hv_done, 1)
                    if k >= 2:
                        kk = k - 2
                        at_least(dve, hhi_done, n * KB + kk + 1)
                        dve.scalar_tensor_tensor(out=hcat[:, kk, T:2 * T], in0=hv[:, kk % 4, :],
                                                 scalar=mods[:, n, 0, kk:kk + 1],
                                                 in1=hcat[:, kk, 0:T].bitcast(F32), op0=ALU.add,
                                                 op1=ALU.subtract).then_inc(hlo_done, 1)

            walk(dve, conv, gated, relu, dt, group, scan, norm, gate)

    return nc


def kernel(x, c, ada_w, ada_b, norm_g, final_g, sc_in_w, sc_conv_w, sc_out_w, m2_in_w, m2_conv_w, m2_conv_b,
           m2_dt_bias, m2_a_log, m2_d, m2_norm_g, m2_out_w, mlp_w1, mlp_w2):
    import concourse.bacc as bacc
    from concourse.bass_utils import run_bass_kernel_spmd

    def slabs(m, order=None):
        m = np.asarray(m).reshape(2, KB // 2, P, -1, P)
        m = m.transpose(3, 0, 2, 1, 4).reshape(-1, 2, P, HALF)
        return m if order is None else m[order]

    def mlp(w1, w2):
        up, parts = slabs(w1), []
        for q in range(4):
            parts += [up[q * KB:(q + 1) * KB], slabs(w2[q * D:(q + 1) * D])]
        return parts

    conv_in = slabs(sc_in_w[0]).reshape(3, KB, 2, P, HALF)
    conv_order = np.stack([conv_in[1], conv_in[2], conv_in[0]], 1).reshape(-1, 2, P, HALF)
    m2 = slabs(m2_in_w[0])
    z0, x0 = 0, DI // P
    b0 = x0 + DI // P
    c0, dt0 = b0 + NG, b0 + 2 * NG

    def groups(lo, hi):
        return m2[[i for g in range(lo, hi) for i in
                   [b0 + g, c0 + g] + [x0 + XB * g + k for k in range(XB)] + [z0 + XB * g + k for k in range(XB)]]]
    units = [conv_order, slabs(sc_out_w[0])] + mlp(mlp_w1[0], mlp_w2[0])
    units += [m2[[dt0]], groups(0, GA), slabs(m2_out_w[0][:D]), groups(GA, NG), slabs(m2_out_w[0][D:])]
    units += mlp(mlp_w1[1], mlp_w2[1])
    w = np.concatenate(units).reshape(2 * UNITS, P, HALF)

    ada = np.asarray(ada_w).reshape(4, D, 3 * KB, P).transpose(0, 2, 3, 1).reshape(ADA, P, D)

    def columns(v):
        v = np.asarray(v)
        v = v.reshape(v.shape[:-1] + (-1, P))
        return np.moveaxis(v, -1, 0)

    taps = np.asarray(m2_conv_w[0]).reshape(-1, P, 3).transpose(1, 0, 2)
    bias = columns(m2_conv_b[0])
    gain = columns(m2_norm_g[0])
    skip = np.repeat(np.asarray(m2_d[0]).reshape(HEADS // 2, 2), HD, axis=1).T
    par = []
    for g in range(NG):
        own = [DI // P + g, DI // P + NG + g] + [XB * g + k for k in range(XB)]
        here = slice(XB * g, XB * g + XB)
        par.append(np.concatenate([taps[:, own].reshape(P, -1), bias[:, own], gain[:, here], skip[:, here]], 1))
    arrays = {
        "w": w,
        "ada": ada,
        "c": np.asarray(c).reshape(D),
        "xT": np.asarray(x[0]).reshape(T, KB, P).transpose(2, 1, 0),
        "adab": columns(np.asarray(ada_b).reshape(-1)),
        "normg": np.concatenate([columns(np.asarray(norm_g).reshape(4, D)), columns(final_g)[:, None]], 1),
        "scw": np.asarray(sc_conv_w[0]).reshape(KB, P, 3).transpose(1, 0, 2),
        "par": np.stack(par, 1),
        "dtb": np.asarray(m2_dt_bias[0]).reshape(P, 1),
        "alog": np.asarray(m2_a_log[0]).reshape(P, 1),
    }
    arrays = {k: np.ascontiguousarray(v) for k, v in arrays.items()}
    nc = bacc.Bacc("TRN2", target_bir_lowering=False, num_devices=1, dynamic_dma_scratch_size=4096)
    ins = {k: nc.dram_tensor("in_" + k, v.shape, F32, kind="ExternalInput").ap() for k, v in arrays.items()}
    out = nc.dram_tensor("out", (P, KB, T), F32, kind="ExternalOutput").ap()
    cum_d = nc.dram_tensor("running_sums", (2, NG, HG, T), F32, kind="Internal").ap()
    build(nc, out=out, cum_d=cum_d, **ins)
    r = run_bass_kernel_spmd(nc, [{"in_" + k: v for k, v in arrays.items()}], core_ids=[0])
    got = r.results[0]["out"]
    return np.ascontiguousarray(got.transpose(2, 1, 0).reshape(1, T, D))
```

```python
from contextlib import ExitStack

import numpy as np

import concourse.bass as bass
from concourse import mybir

P = 128
D = 2048
T = 256
KB = D // P
DI = 4096
HEADS = 64
HD = 64
NG = 8
N = 128
FF = 4 * D
EPS = 1e-6
HG = HEADS // NG
XB = DI // NG // P
HALF = KB // 2 * P

F32 = mybir.dt.float32
F32R = mybir.dt.float32r
ALU = mybir.AluOpType
ACT = mybir.ActivationFunctionType

U_CONV = 0
U_SCOUT = U_CONV + 3 * KB
U_MLP0 = U_SCOUT + KB
U_DT = U_MLP0 + 2 * FF // P
GU = 2 + 2 * XB
U_GA = U_DT + 1
GA = 5
U_OUT0 = U_GA + GA * GU
U_GB = U_OUT0 + KB
U_OUT1 = U_GB + (NG - GA) * GU
U_MLP1 = U_OUT1 + KB
UNITS = U_MLP1 + 2 * FF // P
ADA = 4 * 3 * KB
ADA_FIRST = 2 * KB


DT_AV, DT_TOK, DT_CUM, DT_ALL = 10, 12, 13, 14


class At:

    def __init__(self, c, terms=()):
        self.c, self.terms = c, tuple(terms)

    def __add__(self, k):
        if isinstance(k, At):
            return At(self.c + k.c, self.terms + k.terms)
        return At(self.c + k, self.terms)

    def __sub__(self, k):
        return self + (-k)

    def __mul__(self, k):
        return At(self.c * k, [(r, a * k) for r, a in self.terms])

    def __floordiv__(self, k):
        assert all(a % k == 0 for _, a in self.terms)
        return At(self.c // k, [(r, a // k) for r, a in self.terms])

    def __mod__(self, k):
        assert all(a % k == 0 for _, a in self.terms)
        return self.c % k

    @property
    def v(self):
        out = self.c
        for r, a in self.terms:
            out = r * a + out
        return out


def at_least(e, sem, n):
    if isinstance(n, At):
        if not n.terms and n.c <= 0:
            return
        assert n.c > 0 or not n.terms, n.c
        n = n.v
    if isinstance(n, int) and n <= 0:
        return
    e.wait_ge(sem, n)


def first_unit(g):
    if not g.terms and g.c >= GA:
        return At(U_GB + (g.c - GA) * GU)
    return g * GU + U_GA


def blocks(g):
    return bass.ds((g * XB).v if g.terms else g.c * XB % KB, XB)


def loop(e, n, body):
    if n == 1:
        body(At(0))
    elif n > 1:
        with e.Fori(0, n) as i:
            body(At(0, [(i, 1)]))


def adas(n, ada_at, a):
    out, k = [], 0
    for s in range(n):
        out.append(a + k if s in ada_at else None)
        k += s in ada_at
    return out


def build(nc, w, ada, c, xT, adab, normg, scw, par, dtb, alog, out, cum_d):
    with ExitStack() as ctx:
        def sb(name, shape, dt=F32):
            return ctx.enter_context(nc.sbuf_tensor(name, shape, dt))

        def sem(name):
            return ctx.enter_context(nc.semaphore(name))

        x = sb("x", [P, KB, T])
        hcat = sb("hcat", [P, KB, 2 * T], F32R)
        hid = sb("hid", [P, KB, 2 * T], F32R)
        raw = sb("raw", [P, 4, HALF])
        wh = sb("wh", [P, 4, HALF], F32R)
        wl = sb("wl", [P, 4, HALF], F32R)
        adat = sb("adat", [P, 2, D])
        cond = sb("cond", [P, D])
        ta = sb("ta", [P, 2, T])
        tt = sb("tt", [P, 2, T])
        acc = sb("acc", [P, 2, T])
        th = sb("th", [P, 2, T])
        pad = sb("pad", [P, 2, T + 2])
        normt = sb("normt", [P, 6 * T])
        hv = normt[:, 0:4 * T].rearrange("p (k t) -> p k t", k=4)
        sq = normt[:, 4 * T:6 * T].rearrange("p (k t) -> p k t", k=2)
        ss = sb("ss", [P, T])
        rbc = sb("rbc", [P, T])
        modt = sb("modt", [P, 2])
        modc = sb("modc", [P, ADA])
        modb = sb("modb", [P, ADA])
        mods = sb("mods", [P, 4, 3, KB])
        ng_c = sb("ng_c", [P, 5, KB])
        scw_c = sb("scw_c", [P, KB, 3])
        parall = sb("parall", [P, NG, 32])
        parg = sb("parg", [P, 2, 32])
        dcol = sb("dcol", [P, 4])
        epsc = sb("epsc", [P, 2])
        ones = sb("ones", [P, P])
        ident = sb("ident", [P, P])
        upf = sb("upf", [P, P])
        upb = sb("upb", [P, P])
        dtS = sb("dtS", [P, 2, 2, HEADS])
        ncS = sb("ncS", [P, 2, 2, HEADS])
        dec = sb("dec", [P, 2, 4, 3 * P])
        bT = sb("bT", [P, T])
        avS = bT[:, :].rearrange("p (c r) -> p c r", c=2)
        cT = sb("cT", [P, T])
        xs = sb("xs", [P, 2, XB, T])
        zs = sb("zs", [P, 2, XB, T])
        gf = sb("gf", [P, 3 * P])
        gb = sb("gb", [P, 3 * P])
        xd = sb("xd", [P, 2, 2, HG * HD])
        em = [None, normt[:, :].rearrange("p (k t) -> p k t", k=4), dec[:, 0], dec[:, 1]]
        em.append(em[1])
        ytok = xd[:, 0]
        dgrp = sb("dgrp", [P, 2, 2, HG])
        ngrp = sb("ngrp", [P, 2, 2, HG])

        psm = [ctx.enter_context(nc.psum_tensor(f"psm{i}", [P, 2 * T], F32)) for i in range(2)]
        psy = [ctx.enter_context(nc.psum_tensor(f"psy{i}", [P, 512], F32)) for i in range(2)]
        psr = [ctx.enter_context(nc.psum_tensor(f"psr{i}", [P, 512], F32)) for i in range(4)]

        raw_in = [sem(f"raw_in{i}") for i in range(4)]
        ada_in = [sem(f"ada_in{i}") for i in range(4)]
        small_in, x_in, c_in, out_done = sem("small_in"), sem("x_in"), sem("c_in"), sem("out_done")
        hi_done, lo_done, mm_done = sem("hi_done"), sem("lo_done"), sem("mm_done")
        copied, summed, stored = sem("copied"), sem("summed"), sem("stored")
        ada_done, mod_copied, mods_done, consts, silu_c = sem("ada_done"), sem("mod_copied"), sem("mods_done"), sem("consts"), sem("silu_c")
        pads, halved = sem("pads"), sem("halved")
        sq_done, ss_added, ss_zero, norm_sum = sem("sq_done"), sem("ss_added"), sem("ss_zero"), sem("norm_sum")
        rms_done, eps_in = sem("rms_done"), sem("eps_in")
        hv_done, h_full, hhi_done = sem("hv_done"), sem("h_full"), sem("hhi_done")
        hlo_dve, hlo_pool = sem("hlo_dve"), sem("hlo_pool")
        sc_mid, sc_step, sc_conv, sc_gated, sc_hi = (sem(n) for n in ("sc_mid", "sc_step", "sc_conv", "sc_gated", "sc_hi"))
        relu_done, relu_hi = sem("relu_done"), sem("relu_hi")
        dt_act, dt_dve, dt_pe = sem("dt_act"), sem("dt_dve"), sem("dt_pe")
        cum_out, cb_in = sem("cum_out"), [sem(f"cb_in{i}") for i in range(3)]
        par_in, grp_in = sem("par_in"), sem("grp_in")
        mc_mid, mc_step, mc_conv, tanh_done = sem("mc_mid"), sem("mc_step"), sem("mc_conv"), sem("tanh_done")
        sg_scores, sg_xt, g_ready, xd_ready = sem("sg_scores"), sem("sg_xt"), sem("g_ready"), sem("xd_ready")
        g_copied, seg_done, exp_done = sem("g_copied"), sem("seg_done"), sem("exp_done")
        em_ready, y_head = sem("em_ready"), sem("y_head")
        y_tok, y_back, v_done, vz_done, gsq = sem("y_tok"), sem("y_back"), sem("v_done"), sem("vz_done"), sem("gsq")
        gss, gsum, grms, gu = sem("gss"), sem("gsum"), sem("grms"), sem("gu")
        u_hi, u_lo = sem("u_hi"), sem("u_lo")
        fin, silu_mul = sem("fin"), sem("silu_mul")
        xt_copied = sem("xt_copied")
        rinv, grinv, seg_far = sem("rinv"), sem("grinv"), sem("seg_far")

        block = ctx.enter_context(nc.Block())

        def walk(e, conv, gated, relu, dt, group, scan, norm, gate=lambda n: None, lead=False):
            def bodies(n, f, peel=lead):
                if peel:
                    f(At(0), True)
                    if n > 1:
                        with e.Fori(0, n - 1) as i:
                            f(At(1, [(i, 1)]), False)
                else:
                    loop(e, n, lambda i: f(i, False))

            norm(0)
            bodies(KB // 2, lambda i, f: conv(i * 6 + U_CONV, i * 2, (0, 1, 3, 4), i * 4 + ADA_FIRST, f), True)
            a = ADA_FIRST + 4 * KB // 2
            gate(0)
            bodies(4, lambda i, f: gated(i * 4 + U_SCOUT, 0, i * 4, range(4), i * 4 + a, f, True, None))
            a += KB

            norm(1)
            bodies(4, lambda i, f: relu(i * 4 + U_MLP0, i * 4, i * 4, 1, range(4), i * 4 + a, f))
            a += KB
            gate(1)
            bodies(4, lambda i, f: gated(i * 4 + (U_MLP0 + KB), 1, i * 4, (), None, f, False, At(U_MLP0)))

            def quarter0(q, last):
                u = q * 32 + U_MLP0
                aq = q * 16 + (a - 16)
                loop(e, 4, lambda i: relu(u + i * 4, i * 4, q * 16 + i * 4, 1, (0, 2), aq + i * 2, False))
                bodies(4, lambda i, f: gated(u + i * 4 + KB, 1, i * 4, (0, 2), aq + i * 2 + 8, f, last, u))
            with e.Fori(0, 2) as q:
                quarter0(At(1, [(q, 1)]), False)
            quarter0(At(3), True)
            a += 48

            norm(2)
            dt()

            def g_unit(g):
                return first_unit(g), (4, 5, 8), g * 3 + a
            group(At(0), *g_unit(At(0)))
            with e.Fori(0, 2) as i:
                for k in (1, 2):
                    g = At(k, [(i, 2)])
                    group(g, *g_unit(g))
            gate(2)
            ao = a + 3 * GA
            bodies(4, lambda i, f: gated(i * 4 + U_OUT0, 2, i * 4, (0, 2), i * 2 + ao, f, False, "chunk 0"))
            a += 8
            for k in range(GA, NG):
                group(At(k), *g_unit(At(k)))
            scan(At(NG - 1))
            a += 3 * NG
            bodies(4, lambda i, f: gated(i * 4 + U_OUT1, 2, i * 4, (0, 2), i * 2 + a, f, True, "chunk 1"))
            a += 8

            norm(3)
            assert a + 8 == ADA
            for i in range(2):
                relu(At(i * 4 + U_MLP1), At(i * 4), At(i * 4 + 64), 3, range(4), At(i * 4 + a), lead and i == 0)
            loop(e, 2, lambda i: relu(i * 4 + (U_MLP1 + 8), i * 4 + 8, i * 4 + 72, 3, (), None, False))
            gate(3)
            bodies(4, lambda i, f: gated(i * 4 + (U_MLP1 + KB), 3, i * 4, (), None, f, False, At(U_MLP1)))
            with e.Fori(0, 2) as q:
                q = At(1, [(q, 1)])
                u = q * 32 + U_MLP1
                loop(e, 4, lambda i: relu(u + i * 4, i * 4, q * 16 + i * 4 + 64, 3, (), None, False))
                bodies(4, lambda i, f: gated(u + i * 4 + KB, 3, i * 4, (), None, f, False, u))
            u = At(U_MLP1 + 96)
            loop(e, 4, lambda i: relu(u + i * 4, i * 4, i * 4 + 112, 3, (), None, False))
            bodies(3, lambda i, f: gated(u + i * 4 + KB, 3, i * 4, (), None, f, True, u))
            gated(u + (KB + 12), 3, At(12), (), None, False, True, u)
            norm(4)

        AHEAD = [(y_head, HG), (y_tok, 2), (y_back, 1), (v_done, XB), (grms, 1), (gu, XB), (u_lo, 1)]

        def first_slot(k):
            return adat[:, k, :] if k < 2 else (xs, zs)[k - 2][:, :, :, :].rearrange("p a b t -> p (a b t)")

        @block.sync
        def _(sp):
            def load_half(h):
                if not h.terms and h.c >= 2 * UNITS:
                    return
                at_least(sp, lo_done, h - 3)
                sp.dma_start(raw[:, h % 4, :], w[h.v]).then_inc(raw_in[h % 4], 16)

            def load_ada(a):
                if not a.terms and a.c >= ADA:
                    return
                at_least(sp, ada_done, a - 1)
                sp.dma_start(adat[:, a % 2, :], ada[a.v]).then_inc(ada_in[a % 2], 16)

            def load_first(a):
                if a.terms:
                    at_least(sp, ada_done, a - 3)
                sp.dma_start(first_slot(a % 4), ada[a.v]).then_inc(ada_in[a % 4], 16)

            sp.dma_start(cond[:, :], c.partition_broadcast(P)).then_inc(c_in, 16)
            for a in range(4):
                load_first(At(a))
            for src, dst in ((adab, modb[:, :]), (normg, ng_c[:, :, :]), (scw, scw_c[:, :, :]),
                             (par, parall[:, :, :]), (dtb, dcol[:, 0:1]), (alog, dcol[:, 1:2])):
                sp.dma_start(dst, src).then_inc(small_in, 16)
            sp.dma_start(x[:, :, :], xT).then_inc(x_in, 16)
            loop(sp, ADA_FIRST // 4 - 1, lambda i: [load_first(i * 4 + 4 + k) for k in range(4)])
            for h in range(8):
                load_half(At(h))
            load_ada(At(ADA_FIRST))
            load_ada(At(ADA_FIRST + 1))

            def steps(u, n, ada_at, a):
                k = 0
                for s in range(n):
                    load_half((u + s) * 2 + 8)
                    load_half((u + s) * 2 + 9)
                    if s in ada_at:
                        load_ada(a + (k + 2))
                        k += 1

            def load_sums(g, piece):
                if piece == 1:
                    sp.wait_ge(cum_out, 16)
                    sp.wait_ge(dt_dve, DT_ALL)
                at_least(sp, y_head, g * HG + HG + (2 if piece == 4 else 0))
                src = cum_d.rearrange("d g h t -> g d h t")[g.v][:, 2 * piece - 2:2 * piece, :]
                for d in range(2):
                    sp.dma_start(em[piece][:, 2 * d:2 * d + 2, 0:T], src[d].partition_broadcast(P))\
                        .then_inc(cb_in[piece % 3], 16)

            def scan_loads(g, s):
                for piece in {0: (3,), 3: (4,)}.get(s, ()):
                    load_sums(g, piece)

            def group(g, u, ada_at, a):
                tiles = adas(GU, ada_at, a)
                for s in range(GU):
                    if g.terms or g.c:
                        scan_loads(g - 1, s)
                    if s == GU - 3:
                        load_sums(g, 1)
                        load_sums(g, 2)
                    steps(u + s, 1, (0,) if tiles[s] else (), tiles[s])

            def scan(g):
                for s in range(4):
                    scan_loads(g, s)

            def norm(n):
                if n < 4:
                    return
                for k in range(4):
                    at_least(sp, fin, 4 * (k + 1))
                    sp.dma_start(out[:, 4 * k:4 * k + 4, :], x[:, 4 * k:4 * k + 4, :]).then_inc(out_done, 16)
                sp.wait_ge(out_done, 64)

            walk(sp, lambda u, j, ada_at, a, f: steps(u, 6, ada_at, a),
                 lambda u, layer, n, ada_at, a, f, last, src: steps(u, 4, ada_at, a),
                 lambda u, j, r, layer, ada_at, a, f: steps(u, 4, ada_at, a),
                 lambda: steps(At(U_DT), 1, (), None),
                 group, scan, norm)

        @block.gpsimd
        def _(pool):
            pool.memset(ones[:, :], 1.0).then_inc(consts, 1)
            pool.memset(ident[:, :], 0.0).then_inc(consts, 1)
            pool.memset(ss[:, :], 0.0).then_inc(ss_zero, 1)
            pool.memset(epsc[:, :], EPS).then_inc(eps_in, 1)
            pool.wait_ge(consts, 2)
            pool.affine_select(out=ident[:, :], in_=ident[:, :], compare_op=ALU.not_equal, fill=1.0, base=0,
                               pattern=[[-1, P]], channel_multiplier=1).then_inc(consts, 1)
            pool.affine_select(out=upf[:, :], in_=ones[:, :], compare_op=ALU.is_ge, fill=0.0, base=0,
                               pattern=[[1, P]], channel_multiplier=-1).then_inc(consts, 1)
            pool.affine_select(out=upb[:, :], in_=ones[:, :], compare_op=ALU.is_ge, fill=0.0, base=0,
                               pattern=[[-1, P]], channel_multiplier=1).then_inc(consts, 1)
            for s, n in AHEAD:
                pool.sem_inc(s, n)

            def keep(a):
                if a is not None:
                    at_least(pool, ada_done, a + 1)
                    pool.tensor_copy(modc[:, bass.ds(a.v, 1)], modt[:, a % 2:a % 2 + 1]).then_inc(mod_copied, 1)

            loop(pool, ADA_FIRST // 2, lambda i: [keep(i * 2 + k) for k in range(2)])

            def add_square(m):
                at_least(pool, sq_done, m + 1)
                at_least(pool, ss_added, m)
                pool.tensor_tensor(ss[:, :], ss[:, :], sq[:, m % 2, :], ALU.add).then_inc(ss_added, 1)

            def conv(u, j, ada_at, a, f):
                tiles = adas(6, ada_at, a)
                for k in range(2):
                    jj, v = j + k, u + 3 * k
                    at_least(pool, summed, v + 2)
                    pool.wait_ge(pads, 1)
                    pool.tensor_tensor(pad[:, k, 1:T + 1], tt[:, v % 2, :], tt[:, (v + 1) % 2, :],
                                       ALU.mult).then_inc(stored, 2)
                    at_least(pool, summed, v + 3)
                    at_least(pool, sc_conv, jj + 1)
                    pool.tensor_tensor(acc[:, k, :], tt[:, (v + 2) % 2, :], acc[:, k, :],
                                       ALU.mult).then_inc(sc_gated, 1)
                    at_least(pool, sc_hi, jj + 1)
                    pool.tensor_tensor(hid[:, jj.v, T:2 * T], acc[:, k, :], hid[:, jj.v, 0:T].bitcast(F32),
                                       ALU.subtract).then_inc(stored, 1)
                    for t in tiles[3 * k:3 * k + 3]:
                        keep(t)

            def gated(u, layer, n, ada_at, a, f, last, src):
                tiles = adas(4, ada_at, a)
                for s in range(4):
                    v, nn = u + s, n + s
                    at_least(pool, summed, v + 1)
                    at_least(pool, stored, v)
                    pool.tensor_tensor(x[:, nn.v, :], x[:, nn.v, :], tt[:, v % 2, :], ALU.add).then_inc(stored, 1)
                    keep(tiles[s])
                    if last:
                        add_square(nn + (layer + 1) * KB)

            def relu(u, j, r, layer, ada_at, a, f):
                tiles = adas(4, ada_at, a)
                for s in range(4):
                    v, jj = u + s, j + s
                    at_least(pool, relu_hi, r + (s + 1))
                    pool.tensor_tensor(hid[:, jj.v, T:2 * T], tt[:, v % 2, :], hid[:, jj.v, 0:T].bitcast(F32),
                                       ALU.subtract).then_inc(stored, 1)
                    keep(tiles[s])

            def dt():
                pool.wait_ge(dt_dve, DT_CUM)
                pool.dma_start(cum_d.rearrange("d g h t -> (d g h) t"), hv[:, 0, :]).then_inc(cum_out, 16)

            def unit_store(g, v, s):
                at_least(pool, tanh_done, g * GU + (s + 1))
                at_least(pool, stored, v)
                par2 = g % 2
                if s < 2:
                    at_least(pool, sg_scores, g)
                    src, dst = acc[:, v % 2, :], (bT, cT)[s][:, :]
                else:
                    at_least(pool, u_lo, g)
                    if s < 2 + XB:
                        src, dst = acc[:, v % 2, :], xs[:, par2, s - 2, :]
                    else:
                        src, dst = tt[:, v % 2, :], zs[:, par2, s - 2 - XB, :]
                t = th[:, v % 2, :]
                pool.tensor_tensor(t, t, src, ALU.mult).then_inc(silu_mul, 1)
                at_least(pool, silu_mul, g * GU + (s + 1))
                pool.tensor_tensor(dst, t, src, ALU.add).then_inc(stored, 1)

            def scan_piece(g, s):
                par2 = g % 2
                flat = lambda b, lo, hi: b[:, par2, lo:hi, :].rearrange("p b t -> p (b t)")
                if s == 0:
                    at_least(pool, xt_copied, g * 2 + 2)
                    at_least(pool, grp_in, g * 2 + 2)
                    for d in (1, 0):
                        if d == 0:
                            at_least(pool, xd_ready, g * 2 + 1)
                        src, dst = (xd[:, i, :, :].rearrange("p c (h e) -> p c h e", e=HD) for i in (0, d))
                        pool.tensor_tensor(dst, src, dgrp[:, :, d, :].unsqueeze(3).to_broadcast([P, 2, HG, HD]),
                                           ALU.mult).then_inc(xd_ready, 1)
                if s == 6:
                    at_least(pool, v_done, g * XB + 2 * XB)
                    at_least(pool, stored, first_unit(g) + GU)
                    pool.tensor_tensor(flat(xs, 0, XB), flat(xs, 0, XB), flat(zs, 0, XB), ALU.mult)\
                        .then_inc(vz_done, 1)
                if s == 7:
                    at_least(pool, gsq, g + 1)
                    pool.tensor_tensor(flat(zs, 0, 2), flat(zs, 0, 2), flat(zs, 2, 4), ALU.add).then_inc(gss, 1)
                    at_least(pool, gss, g * 2 + 1)
                    pool.tensor_tensor(flat(zs, 0, 1), flat(zs, 0, 1), flat(zs, 1, 2), ALU.add).then_inc(gss, 1)

            def scan_late(g, s):
                if s == 9:
                    at_least(pool, u_hi, g + 1)
                    pool.tensor_tensor(hid[:, blocks(g), T:2 * T], xs[:, g % 2, :, :],
                                       hid[:, blocks(g), 0:T].bitcast(F32), ALU.subtract).then_inc(u_lo, 1)

            def group(g, u, ada_at, a):
                at_least(pool, gu, g * XB)
                pool.wait_ge(halved, 1)
                pool.tensor_copy(parg[:, g % 2, :], parall[:, g.v, :]).then_inc(par_in, 1)
                tiles = adas(GU, ada_at, a)
                for s in range(GU):
                    if g.terms or g.c:
                        scan_piece(g - 1, s)
                    unit_store(g, u + s, s)
                    keep(tiles[s])
                    if g.terms or g.c:
                        scan_late(g - 1, s)

            def scan(g):
                for s in range(10):
                    scan_piece(g, s)
                    scan_late(g, s)

            def norm(n):
                if n == 0:
                    for m in range(KB):
                        if m == 0:
                            pool.wait_ge(ss_zero, 1)
                        add_square(At(m))
                at_least(pool, norm_sum, n + 1)
                pool.memset(ss[:, :], 0.0).then_inc(ss_zero, 1)
                at_least(pool, ss_zero, n + 2)
                if n < 4:
                    for k in range(1, KB, 2):
                        at_least(pool, hhi_done, n * KB + k + 1)
                        pool.tensor_tensor(hcat[:, k, T:2 * T], hv[:, k % 4, :], hcat[:, k, 0:T].bitcast(F32),
                                           ALU.subtract).then_inc(hlo_pool, 1)

            walk(pool, conv, gated, relu, dt, group, scan, norm)

        @block.scalar
        def _(act):
            def hi(h):
                if not h.terms and h.c >= 2 * UNITS:
                    return
                at_least(act, raw_in[h % 4], (h - h % 4) * 4 + 16)
                at_least(act, mm_done, h - 3)
                act.activation(wh[:, h % 4, :], raw[:, h % 4, :], ACT.Copy).then_inc(hi_done, 1)

            def copy(v, scale=1.0):
                at_least(act, mm_done, v * 2 + 2)
                at_least(act, summed, v - 1)
                act.activation(ta[:, v % 2, :], psm[v % 2][:, 0:T], ACT.Copy, scale=scale).then_inc(copied, 1)

            def square(m, src):
                at_least(act, ss_added, m - 1)
                act.activation(sq[:, m % 2, :], src, ACT.Square).then_inc(sq_done, 1)

            def step(v, scale=1.0):
                hi(v * 2 + 4)
                copy(v, scale)
                hi(v * 2 + 5)

            act.wait_ge(c_in, 16)
            act.activation(cond[:, :], cond[:, :], ACT.Silu).then_inc(silu_c, 1)
            for h in range(4):
                hi(At(h))

            def conv(u, j, ada_at, a, f):
                for k in range(2):
                    jj, v = j + k, u + 3 * k
                    step(v)
                    step(v + 1)
                    at_least(act, stored, v + 2)
                    act.activation(acc[:, k, :], pad[:, k, 1:T + 1], ACT.Copy,
                                   scale=scw_c[:, jj.v, 1:2]).then_inc(sc_mid, 1)
                    step(v + 2)
                    at_least(act, sc_gated, jj + 1)
                    act.activation(hid[:, jj.v, 0:T], acc[:, k, :], ACT.Copy).then_inc(sc_hi, 1)

            def gated(u, layer, n, ada_at, a, f, last, src):
                at_least(act, mods_done, 4 * layer + 4)
                for s in range(4):
                    v, nn = u + s, n + s
                    step(v, mods[:, layer, 2, bass.ds(nn.v, 1)])
                    if last:
                        at_least(act, stored, v + 1)
                        square(nn + (layer + 1) * KB, x[:, nn.v, :])

            def relu(u, j, r, layer, ada_at, a, f):
                for s in range(4):
                    v, jj = u + s, j + s
                    step(v)
                    at_least(act, relu_done, r + (s + 1))
                    act.activation(hid[:, jj.v, 0:T], tt[:, v % 2, :], ACT.Copy).then_inc(relu_hi, 1)

            def dt():
                v = At(U_DT)
                step(v)
                at_least(act, summed, v + 1)
                act.activation(th[:, 0, :], tt[:, v % 2, :], ACT.Abs, bias=dcol[:, 0:1]).then_inc(dt_act, 1)
                act.wait_ge(dt_act, 1)
                act.activation(th[:, 0, :], th[:, 0, :], ACT.Exp, scale=-1.0).then_inc(dt_act, 1)
                act.activation(dcol[:, 2:3], dcol[:, 1:2], ACT.Exp).then_inc(dt_act, 1)
                act.wait_ge(dt_dve, 1)
                act.activation(hv[:, 0, :], hv[:, 1, :], ACT.Ln).then_inc(dt_act, 1)

            def unit(g, v, s, scanning):
                conv_unit = s < 2 + XB
                if scanning:
                    scanning()
                hi(v * 2 + 4)
                copy(v, 1.0 if conv_unit else 0.5)
                hi(v * 2 + 5)
                par2 = g % 2
                if conv_unit:
                    at_least(act, summed, v + 1)
                    at_least(act, par_in, g + 1)
                    at_least(act, stored, v - 1)
                    act.activation(acc[:, v % 2, :], pad[:, v % 2, 1:T + 1], ACT.Identity,
                                   bias=parg[:, par2, 18 + s:19 + s],
                                   scale=parg[:, par2, 3 * s + 1:3 * s + 2]).then_inc(mc_mid, 1)
                    at_least(act, mc_conv, g * 6 + (s + 1))
                    act.activation(th[:, v % 2, :], acc[:, v % 2, :], ACT.Tanh).then_inc(tanh_done, 1)
                else:
                    at_least(act, summed, v + 1)
                    at_least(act, stored, v - 1)
                    act.activation(th[:, v % 2, :], tt[:, v % 2, :], ACT.Tanh).then_inc(tanh_done, 1)

            def scan_piece(g, s):
                par2 = g % 2
                if s == 0:
                    at_least(act, sg_scores, g + 1)
                    at_least(act, y_head, g * HG + HG)
                    act.activation(gf[:, P:T], psr[0][:, P:T], ACT.Copy).then_inc(g_copied, 1)
                    act.activation(gb[:, 0:P], psr[0][:, T:T + P], ACT.Copy).then_inc(g_copied, 1)
                    at_least(act, sg_xt, g + 1)
                    at_least(act, y_back, g + 1)
                    for ch in range(2):
                        act.activation(xd[:, 0, ch, :], psy[ch][:, :], ACT.Copy).then_inc(xt_copied, 1)
                if s == 5:
                    at_least(act, y_head, g * HG + 2 * HG)
                    for ch in range(2):
                        act.activation(ytok[:, ch, :], psy[ch][:, :], ACT.Copy).then_inc(y_tok, 1)
                if s == 7:
                    at_least(act, vz_done, g + 1)
                    act.activation(zs[:, par2, :, :], xs[:, par2, :, :], ACT.Square).then_inc(gsq, 1)
                if s == 9:
                    at_least(act, gsum, g + 1)
                    act.activation(rbc[:, :], psr[2][:, 0:T], ACT.Sqrt, bias=epsc[:, 0:1],
                                   scale=1.0 / (XB * P)).then_inc(grms, 1)

            def decays(g, piece):
                at_least(act, seg_done, g * 4 + piece)
                act.activation(em[piece], em[piece], ACT.Exp).then_inc(exp_done, 1)

            def scan_late(g, s):
                par2 = g % 2
                if s in (0, 1, 3):
                    decays(g, {0: 2, 1: 3, 3: 4}[s])
                if s == 9:
                    at_least(act, gu, g * XB + 2 * XB)
                    act.activation(hid[:, blocks(g), 0:T], xs[:, par2, :, :], ACT.Copy).then_inc(u_hi, 1)

            def group(g, u, ada_at, a):
                for s in range(GU):
                    scanning = (lambda s=s: scan_piece(g - 1, s)) if g.terms or g.c else None
                    unit(g, u + s, s, scanning)
                    if scanning:
                        scan_late(g - 1, s)
                decays(g, 1)

            def scan(g):
                for s in range(10):
                    scan_piece(g, s)
                    scan_late(g, s)

            def norm(n):
                if n == 0:
                    act.wait_ge(eps_in, 1)
                    act.wait_ge(x_in, 16)
                    for m in range(KB):
                        square(At(m), x[:, m, :])
                act.activation(epsc[:, 1:2], epsc[:, 0:1], ACT.Sqrt)
                at_least(act, norm_sum, n + 1)
                act.activation(rbc[:, :], psr[2][:, 0:T], ACT.Sqrt, bias=epsc[:, 0:1],
                               scale=1.0 / D).then_inc(rms_done, 1)
                if n == 4:
                    return
                at_least(act, mods_done, 4 * n + 3)
                for k in range(KB):
                    at_least(act, hv_done, n * KB + k + 1)
                    h, hi_out, shift = hv[:, k % 4, :], hcat[:, k, 0:T], mods[:, n, 0, k:k + 1]
                    if k % 2 == 0:
                        act.activation(hi_out, h, ACT.Identity, bias=shift).then_inc(hhi_done, 1)
                    else:
                        act.activation(h, h, ACT.Identity, bias=shift).then_inc(h_full, 1)
                        at_least(act, h_full, n * KB // 2 + k // 2 + 1)
                        act.activation(hi_out, h, ACT.Copy).then_inc(hhi_done, 1)

            walk(act, conv, gated, relu, dt, group, scan, norm)

        @block.tensor
        def _(pe):
            def unit(u, src, ready=None):
                bank = psm[u % 2]
                for half in range(2):
                    h = u * 2 + half
                    at_least(pe, lo_done, h + 1)
                    if half == 0:
                        at_least(pe, summed, u - 1)
                    for k in range(KB // 2):
                        kb = half * KB // 2 + k
                        if ready:
                            ready(kb)
                        pe.matmul(bank[:, :], wh[:, h % 4, k * P:(k + 1) * P], src[:, kb, :],
                                  start=(kb == 0), stop=(kb == KB - 1), skip_group_check=True)
                        mm = pe.matmul(bank[:, T:2 * T], wl[:, h % 4, k * P:(k + 1) * P], src[:, kb, 0:T],
                                       start=False, stop=(kb == KB - 1), skip_group_check=True)
                    mm.then_inc(mm_done, 1)

            def norm_ready(n):
                return lambda kb: at_least(pe, (hlo_dve, hlo_pool)[kb % 2], (n * KB + kb) // 2 + 1)

            def pair(u, ready):
                at_least(pe, lo_done, u * 2 + 4)
                at_least(pe, summed, u)
                for kb in range(KB):
                    ready(kb)
                    for i in range(2):
                        bank, h = psm[(u + i) % 2], (u + i) * 2 + kb // (KB // 2)
                        k = kb % (KB // 2)
                        pe.matmul(bank[:, :], wh[:, h % 4, k * P:(k + 1) * P], hcat[:, kb, :],
                                  start=(kb == 0), stop=(kb == KB - 1), skip_group_check=True)
                        mm = pe.matmul(bank[:, T:2 * T], wl[:, h % 4, k * P:(k + 1) * P], hcat[:, kb, 0:T],
                                       start=False, stop=(kb == KB - 1), skip_group_check=True)
                    if kb == KB // 2 - 1:
                        mm.then_inc(mm_done, 1)
                mm.then_inc(mm_done, 3)

            def conv(u, j, ada_at, a, first):
                if first:
                    pair(u, norm_ready(0))
                for s in range(2 if first else 0, 6):
                    unit(u + s, hcat)

            def gated(u, layer, n, ada_at, a, first, last, src):
                def ready(kb):
                    if src in ("chunk 0", "chunk 1"):
                        if kb % XB == 0:
                            at_least(pe, u_lo, kb // XB + (2 if src == "chunk 0" else 2 + NG // 2))
                    elif isinstance(src, At):
                        at_least(pe, stored, src + (kb + 1))
                    else:
                        at_least(pe, stored, 3 * (kb + 1))
                for s in range(4):
                    unit(u + s, hid, ready if first and s == 0 else None)

            def relu(u, j, r, layer, ada_at, a, first):
                if first:
                    pair(u, norm_ready(layer))
                for s in range(2 if first else 0, 4):
                    unit(u + s, hcat)

            def dt():
                unit(At(U_DT), hcat, norm_ready(2))
                pe.wait_ge(consts, 5)
                pe.wait_ge(dt_dve, DT_AV)
                for i, src in ((0, acc[:, 0, :]), (1, acc[:, 1, :])):
                    for ch in range(2):
                        mm = pe.transpose(psr[i][:, ch * P:(ch + 1) * P], src[:, ch * P:(ch + 1) * P], ident[:, :])
                mm.then_inc(dt_pe, 1)
                pe.wait_ge(dt_dve, DT_TOK)
                f, b = slice(0, HEADS), slice(HEADS, P)
                for rows, up, near, far in ((f, upf, 0, 1), (b, upb, 1, 0)):
                    pe.matmul(psr[2][rows, near * P:(near + 1) * P], avS[:, near, rows], up[:, :],
                              start=True, stop=True, skip_group_check=True)
                    pe.matmul(psr[2][rows, far * P:(far + 1) * P], avS[:, near, rows], ones[:, :],
                              start=False, stop=False, skip_group_check=True)
                    mm = pe.matmul(psr[2][rows, far * P:(far + 1) * P], avS[:, far, rows], up[:, :],
                                   start=False, stop=True, skip_group_check=True)
                mm.then_inc(dt_pe, 1)
                pe.wait_ge(dt_dve, DT_CUM)
                for ch in range(2):
                    mm = pe.transpose(psr[3][:, ch * P:(ch + 1) * P], hv[:, 0, ch * P:(ch + 1) * P], ident[:, :])
                mm.then_inc(dt_pe, 1)

            def scan_piece(g, s):
                par2 = g % 2
                if s == 0:
                    at_least(pe, stored, first_unit(g) + 2 + XB)
                    at_least(pe, v_done, g * XB + XB)
                    at_least(pe, dt_dve, DT_ALL)
                    for ch in range(2):
                        mm = pe.matmul(psr[0][:, ch * T:(ch + 1) * T], bT[:, ch * P:(ch + 1) * P], cT[:, :],
                                       start=True, stop=True, skip_group_check=True)
                    mm.then_inc(sg_scores, 1)
                    at_least(pe, y_tok, g * 2 + 2)
                    for ch in range(2):
                        for b in range(XB):
                            mm = pe.transpose(psy[ch][:, b * P:(b + 1) * P], xs[:, par2, b, ch * P:(ch + 1) * P],
                                              ident[:, :])
                    mm.then_inc(sg_xt, 1)
                if 2 <= s <= 5:
                    for h in (2 * (s - 2), 2 * (s - 2) + 1):
                        if h == 0:
                            at_least(pe, xd_ready, g * 2 + 2)
                        at_least(pe, em_ready, g * 4 + (s - 1))
                        mf, mb = em[s - 1][:, h % 2, :], em[s - 1][:, 2 + h % 2, :]
                        cols = slice(h * HD, (h + 1) * HD)
                        for ch, terms in ((0, ((mf, 0, 0, 0), (mb, 2 * P, 1, 0), (mb, 0, 1, 1))),
                                          (1, ((mf, P, 0, 0), (mf, 2 * P, 0, 1), (mb, P, 1, 1)))):
                            for i, (m, at, d, sc) in enumerate(terms):
                                mm = pe.matmul(psy[ch][:, cols], m[:, at:at + P], xd[:, d, sc, cols],
                                               start=(i == 0), stop=(i == 2), skip_group_check=True)
                        mm.then_inc(y_head, 1)
                if s == 6:
                    at_least(pe, y_tok, g * 2 + 4)
                    at_least(pe, g_ready, g * 4 + 4)
                    for b in range(XB):
                        for ch in range(2):
                            at = (b % 2) * T + ch * P
                            mm = pe.transpose(psr[b // 2][:, at:at + P], ytok[:, ch, b * P:(b + 1) * P],
                                              ident[:, :])
                    mm.then_inc(y_back, 1)
                if s == 9:
                    at_least(pe, gss, g * 2 + 2)
                    at_least(pe, grms, g + 1)
                    pe.matmul(psr[2][:, 0:T], ones[:, :], zs[:, par2, 0, :], start=True, stop=True,
                              skip_group_check=True).then_inc(gsum, 1)

            def group(g, u, ada_at, a):
                for s in range(GU):
                    if g.terms or g.c:
                        scan_piece(g - 1, s)
                    unit(u + s, hcat)

            def scan(g):
                for s in range(10):
                    scan_piece(g, s)

            def norm(n):
                if n == 0:
                    pe.wait_ge(consts, 5)
                at_least(pe, ss_added, KB * (n + 1))
                if n == 3:
                    at_least(pe, grms, NG + 1)
                pe.matmul(psr[2][:, 0:T], ones[:, :], ss[:, :], start=True, stop=True,
                          skip_group_check=True).then_inc(norm_sum, 1)

            walk(pe, conv, gated, relu, dt, group, scan, norm, lead=True)

        @block.vector
        def _(dve):
            def lo(h):
                if not h.terms and h.c >= 2 * UNITS:
                    return
                at_least(dve, hi_done, h + 1)
                dve.tensor_tensor(wl[:, h % 4, :], raw[:, h % 4, :], wh[:, h % 4, :].bitcast(F32),
                                  ALU.subtract).then_inc(lo_done, 1)

            def tile(a, first=False):
                if first:
                    at_least(dve, ada_in[a % 4], (a - a % 4) * 4 + 16)
                    t = first_slot(a % 4)
                else:
                    at_least(dve, ada_in[a % 2], (a - a % 2 - ADA_FIRST) * 8 + (ADA_FIRST * 4 + 16))
                    t = adat[:, a % 2, :]
                at_least(dve, mod_copied, a - 1)
                dve.tensor_tensor_reduce(t, t, cond[:, :], 1.0, 0.0, ALU.mult, ALU.add,
                                         modt[:, a % 2:a % 2 + 1]).then_inc(ada_done, 1)

            def step(v, add, rest=None, ada=None, scanning=None):
                if scanning:
                    scanning()
                lo(v * 2 + 4)
                at_least(dve, copied, v + 1)
                add(v).then_inc(summed, 1)
                lo(v * 2 + 5)
                if rest:
                    rest()
                if ada is not None:
                    tile(ada)

            def add_tt(v):
                at_least(dve, stored, v - 1)
                return dve.tensor_tensor(tt[:, v % 2, :], ta[:, v % 2, :], psm[v % 2][:, T:2 * T], ALU.add)

            def modulation(n, which):
                at_least(dve, mod_copied, 3 * KB * n + KB * (which + 1))
                cols = slice(3 * KB * n + KB * which, 3 * KB * n + KB * (which + 1))
                dve.tensor_tensor(mods[:, n, which, :], modc[:, cols], modb[:, cols], ALU.add).then_inc(mods_done, 1)
                if which == 1:
                    at_least(dve, mods_done, 4 * n + 2)
                    dve.scalar_tensor_tensor(out=mods[:, n, 1, :], in0=mods[:, n, 1, :], scalar=1.0,
                                             in1=ng_c[:, n, :], op0=ALU.add, op1=ALU.mult).then_inc(mods_done, 1)

            dve.memset(pad[:, :, :], 0.0).then_inc(pads, 1)
            dve.wait_ge(small_in, 96)
            dve.tensor_scalar(parall[:, :, 0:24], parall[:, :, 0:24], 0.5, None, ALU.mult).then_inc(halved, 1)
            dve.wait_ge(silu_c, 1)
            for a in range(4):
                tile(At(a), True)
            loop(dve, ADA_FIRST // 4 - 1, lambda i: [tile(i * 4 + 4 + k, True) for k in range(4)])
            for h in range(4):
                lo(At(h))

            def conv(u, j, ada_at, a, f):
                tiles = adas(6, ada_at, a)
                for k in range(2):
                    jj, v = j + k, u + 3 * k
                    step(v, add_tt, None, tiles[3 * k])
                    step(v + 1, add_tt, None, tiles[3 * k + 1])

                    def taps():
                        at_least(dve, sc_mid, jj + 1)
                        dve.scalar_tensor_tensor(out=acc[:, k, :], in0=pad[:, k, 0:T], scalar=scw_c[:, jj.v, 0:1],
                                                 in1=acc[:, k, :], op0=ALU.mult, op1=ALU.add).then_inc(sc_step, 1)
                        at_least(dve, sc_step, jj + 1)
                        dve.scalar_tensor_tensor(out=acc[:, k, :], in0=pad[:, k, 2:T + 2],
                                                 scalar=scw_c[:, jj.v, 2:3], in1=acc[:, k, :], op0=ALU.mult,
                                                 op1=ALU.add).then_inc(sc_conv, 1)
                    step(v + 2, add_tt, taps, tiles[3 * k + 2])

            def gate(layer):
                modulation(layer, 2)

            def gated(u, layer, n, ada_at, a, f, last, src):
                tiles = adas(4, ada_at, a)

                for s in range(4):
                    nn = n + s
                    gcol = mods[:, layer, 2, bass.ds(nn.v, 1)]

                    def add(v):
                        at_least(dve, stored, v - 1)
                        return dve.scalar_tensor_tensor(out=tt[:, v % 2, :], in0=psm[v % 2][:, T:2 * T], scalar=gcol,
                                                        in1=ta[:, v % 2, :], op0=ALU.mult, op1=ALU.add)
                    step(u + s, add, None, tiles[s])

            def relu(u, j, r, layer, ada_at, a, f):
                tiles = adas(4, ada_at, a)
                for s in range(4):
                    v = u + s

                    def square():
                        at_least(dve, summed, v + 1)
                        t = tt[:, v % 2, :]
                        dve.scalar_tensor_tensor(out=t, in0=t, scalar=0.0, in1=t, op0=ALU.max,
                                                 op1=ALU.mult).then_inc(relu_done, 1)
                    step(v, add_tt, square, tiles[s])

            def dt():
                v = At(U_DT)
                step(v, add_tt)
                n = [0]

                def own(ins):
                    n[0] += 1
                    ins.then_inc(dt_dve, 1)

                e, e1, m, r = th[:, 0, :], hv[:, 1, :], hv[:, 2, :], hv[:, 3, :]
                dve.wait_ge(dt_act, 2)
                own(dve.tensor_scalar(e1, e, 1.0, None, ALU.add))
                dve.wait_ge(dt_dve, 1)
                own(dve.tensor_scalar(r, e1, -1.0, None, ALU.add))
                dve.wait_ge(dt_dve, 2)
                own(dve.tensor_scalar(m, r, 0.0, None, ALU.is_equal))
                dve.wait_ge(dt_dve, 3)
                own(dve.tensor_tensor(r, r, m, ALU.add))
                dve.wait_ge(dt_dve, 4)
                own(dve.reciprocal(r, r))
                dve.wait_ge(dt_dve, 5)
                own(dve.tensor_tensor(r, r, e, ALU.mult))
                dve.wait_ge(dt_act, 4)
                own(dve.tensor_tensor(m, m, hv[:, 0, :], ALU.add))
                dve.wait_ge(dt_dve, 7)
                own(dve.tensor_tensor(r, r, m, ALU.mult))
                own(dve.tensor_scalar(acc[:, 0, :], tt[:, v % 2, :], dcol[:, 0:1], 0.0, ALU.add, ALU.max))
                dve.wait_ge(dt_dve, 9)
                at_least(dve, stored, v)
                dve.tensor_tensor(acc[:, 0, :], acc[:, 0, :], r, ALU.add).then_inc(stored, 1)
                at_least(dve, stored, v + 1)
                own(dve.tensor_scalar(acc[:, 1, :], acc[:, 0, :], dcol[:, 2:3], -1.0, ALU.mult, ALU.mult))
                assert n[0] == DT_AV
                dve.wait_ge(dt_pe, 1)
                own(dve.tensor_copy(dtS[:, :, :, :].rearrange("p c d h -> p (c d h)"), psr[0][:, 0:T]))
                own(dve.tensor_copy(avS[:, :, :].rearrange("p c r -> p (c r)"), psr[1][:, 0:T]))
                assert n[0] == DT_TOK
                dve.wait_ge(dt_pe, 2)
                own(dve.tensor_copy(hv[:, 0, :], psr[2][:, 0:T]))
                assert n[0] == DT_CUM
                dve.wait_ge(dt_pe, 3)
                own(dve.tensor_scalar(ncS[:, :, :, :].rearrange("p c d h -> p (c d h)"), psr[3][:, 0:T], -1.0, None,
                                      ALU.mult))
                assert n[0] == DT_ALL

            def unit(g, v, s, ada, scanning):
                par2 = g % 2
                if s < 2 + XB:
                    def add(v):
                        at_least(dve, mc_conv, g * 6 + (s - 1))
                        return dve.tensor_tensor(pad[:, v % 2, 1:T + 1], ta[:, v % 2, :], psm[v % 2][:, T:2 * T],
                                                 ALU.add)

                    def taps():
                        a = acc[:, v % 2, :]
                        at_least(dve, mc_mid, g * 6 + (s + 1))
                        dve.scalar_tensor_tensor(out=a, in0=pad[:, v % 2, 0:T], scalar=parg[:, par2, 3 * s:3 * s + 1],
                                                 in1=a, op0=ALU.mult, op1=ALU.add).then_inc(mc_step, 1)
                        at_least(dve, mc_step, g * 6 + (s + 1))
                        dve.scalar_tensor_tensor(out=a, in0=pad[:, v % 2, 2:T + 2],
                                                 scalar=parg[:, par2, 3 * s + 2:3 * s + 3], in1=a, op0=ALU.mult,
                                                 op1=ALU.add).then_inc(mc_conv, 1)
                    step(v, add, taps, ada, scanning)
                else:
                    def add(v):
                        at_least(dve, stored, v - 1)
                        return dve.scalar_tensor_tensor(out=tt[:, v % 2, :], in0=psm[v % 2][:, T:2 * T], scalar=0.5,
                                                        in1=ta[:, v % 2, :], op0=ALU.mult, op1=ALU.add)
                    step(v, add, None, ada, scanning)

            def scan_piece(g, s):
                par2 = g % 2
                if s == 0:
                    at_least(dve, y_head, g * HG + HG)
                    at_least(dve, g_copied, g * 2 + 2)
                    for dst, at, src, up in ((gf, 0, 0, upf), (gf, T, T + P, upf), (gb, P, T + P, upb), (gb, T, 0, upb)):
                        dve.tensor_tensor(dst[:, at:at + P], psr[0][:, src:src + P], up[:, :], ALU.mult)\
                            .then_inc(g_ready, 1)
                if s in (0, 1, 2, 4):
                    piece = {0: 1, 1: 2, 2: 3, 4: 4}[s]
                    if s == 0:
                        at_least(dve, g_ready, g * 4 + 4)
                    at_least(dve, exp_done, g * 4 + piece)
                    for d, scores in enumerate((gf, gb)):
                        m = em[piece][:, 2 * d:2 * d + 2, :]
                        ins = dve.tensor_tensor(m, m, scores[:, :].unsqueeze(1).to_broadcast([P, 2, 3 * P]), ALU.mult)
                    ins.then_inc(em_ready, 1)
                if s == 6:
                    at_least(dve, y_back, g + 2)
                    for b in range(XB):
                        v = xs[:, par2, b, :]
                        dve.scalar_tensor_tensor(out=v, in0=v, scalar=parg[:, par2, 28 + b:29 + b],
                                                 in1=psr[b // 2][:, (b % 2) * T:(b % 2) * T + T],
                                                 op0=ALU.mult, op1=ALU.add).then_inc(v_done, 1)
                if s == 9:
                    at_least(dve, grms, g + 2)
                    dve.reciprocal(rbc[:, :], rbc[:, :]).then_inc(grinv, 1)
                    at_least(dve, grinv, g + 1)
                    for b in range(XB):
                        v = xs[:, par2, b, :]
                        dve.scalar_tensor_tensor(out=v, in0=v, scalar=parg[:, par2, 24 + b:25 + b], in1=rbc[:, :],
                                                 op0=ALU.mult, op1=ALU.mult).then_inc(gu, 1)

            def columns_of(g):
                at_least(dve, dt_dve, DT_ALL)
                at_least(dve, xd_ready, g * 2)
                at_least(dve, seg_done, g * 4)
                for dst, src in ((ngrp, ncS), (dgrp, dtS)):
                    cols = src[:, :, :, :].rearrange("p c d (g h) -> p c d g h", g=NG)
                    dve.tensor_copy(dst[:, :, :, :], cols[:, :, :, g.v, :]).then_inc(grp_in, 1)

            def segments(g, s):
                at_least(dve, cb_in[s % 3], g * 64 + (32 if s == 1 else 64) if s % 3 == 1 else g * 32 + 32)
                if s == 1:
                    at_least(dve, grp_in, g * 2 + 2)
                rows = [(d, em[s][:, 2 * d + i, :], 2 * (s - 1) + i) for d in range(2) for i in range(2)]
                for d, row, h in rows:
                    far = slice(P, T) if d == 0 else slice(0, P)
                    ins = dve.tensor_scalar(row[:, T:3 * P], row[:, far], ngrp[:, 1 - d, d, h:h + 1], 0.0,
                                            ALU.add, ALU.min)
                ins.then_inc(seg_far, 1)
                at_least(dve, seg_far, g * 4 + s)
                for d, row, h in rows:
                    ins = dve.tensor_scalar(row[:, 0:T], row[:, 0:T], ngrp[:, d, d, h:h + 1], 0.0, ALU.add, ALU.min)
                ins.then_inc(seg_done, 1)

            def group(g, u, ada_at, a):
                tiles = adas(GU, ada_at, a)
                for s in range(GU):
                    scanning = None
                    if g.terms or g.c:
                        scanning = lambda s=s: scan_piece(g - 1, s)
                    unit(g, u + s, s, tiles[s], scanning)
                    if scanning and s in (0, 1, 3):
                        segments(g - 1, {0: 2, 1: 3, 3: 4}[s])
                columns_of(g)
                segments(g, 1)

            def scan(g):
                for s in range(10):
                    scan_piece(g, s)
                    if s in (0, 1, 3):
                        segments(g, {0: 2, 1: 3, 3: 4}[s])

            def norm(n):
                if n < 4:
                    modulation(n, 0)
                    modulation(n, 1)
                at_least(dve, rms_done, n + 1)
                dve.reciprocal(rbc[:, :], rbc[:, :]).then_inc(rinv, 1)
                at_least(dve, rinv, n + 1)
                if n == 4:
                    for k in range(KB):
                        dve.scalar_tensor_tensor(out=x[:, k, :], in0=x[:, k, :], scalar=ng_c[:, 4, k:k + 1],
                                                 in1=rbc[:, :], op0=ALU.mult, op1=ALU.mult).then_inc(fin, 1)
                    return
                at_least(dve, mods_done, 4 * n + 3)
                for k in range(KB + 2):
                    if k < KB:
                        if k >= 4:
                            at_least(dve, (hlo_dve, hlo_pool)[k % 2], (n * KB + k - 4) // 2 + 1)
                        dve.scalar_tensor_tensor(out=hv[:, k % 4, :], in0=x[:, k, :], scalar=mods[:, n, 1, k:k + 1],
                                                 in1=rbc[:, :], op0=ALU.mult, op1=ALU.mult).then_inc(hv_done, 1)
                    kk = k - 2
                    if kk >= 0 and kk % 2 == 0:
                        at_least(dve, hhi_done, n * KB + kk + 1)
                        dve.scalar_tensor_tensor(out=hcat[:, kk, T:2 * T], in0=hv[:, kk % 4, :],
                                                 scalar=mods[:, n, 0, kk:kk + 1],
                                                 in1=hcat[:, kk, 0:T].bitcast(F32), op0=ALU.add,
                                                 op1=ALU.subtract).then_inc(hlo_dve, 1)

            walk(dve, conv, gated, relu, dt, group, scan, norm, gate)

    return nc


def kernel(x, c, ada_w, ada_b, norm_g, final_g, sc_in_w, sc_conv_w, sc_out_w, m2_in_w, m2_conv_w, m2_conv_b,
           m2_dt_bias, m2_a_log, m2_d, m2_norm_g, m2_out_w, mlp_w1, mlp_w2):
    import concourse.bacc as bacc
    from concourse.bass_utils import run_bass_kernel_spmd

    def slabs(m, order=None):
        m = np.asarray(m).reshape(2, KB // 2, P, -1, P)
        m = m.transpose(3, 0, 2, 1, 4).reshape(-1, 2, P, HALF)
        return m if order is None else m[order]

    def mlp(w1, w2):
        up, parts = slabs(w1), []
        for q in range(4):
            parts += [up[q * KB:(q + 1) * KB], slabs(w2[q * D:(q + 1) * D])]
        return parts

    conv_in = slabs(sc_in_w[0]).reshape(3, KB, 2, P, HALF)
    conv_order = np.stack([conv_in[1], conv_in[2], conv_in[0]], 1).reshape(-1, 2, P, HALF)
    m2 = slabs(m2_in_w[0])
    z0, x0 = 0, DI // P
    b0 = x0 + DI // P
    c0, dt0 = b0 + NG, b0 + 2 * NG

    def groups(lo, hi):
        return m2[[i for g in range(lo, hi) for i in
                   [b0 + g, c0 + g] + [x0 + XB * g + k for k in range(XB)] + [z0 + XB * g + k for k in range(XB)]]]
    units = [conv_order, slabs(sc_out_w[0])] + mlp(mlp_w1[0], mlp_w2[0])
    units += [m2[[dt0]], groups(0, GA), slabs(m2_out_w[0][:D]), groups(GA, NG), slabs(m2_out_w[0][D:])]
    units += mlp(mlp_w1[1], mlp_w2[1])
    w = np.concatenate(units).reshape(2 * UNITS, P, HALF)

    ada = np.asarray(ada_w).reshape(4, D, 3 * KB, P).transpose(0, 2, 3, 1).reshape(ADA, P, D)

    def columns(v):
        v = np.asarray(v)
        v = v.reshape(v.shape[:-1] + (-1, P))
        return np.moveaxis(v, -1, 0)

    taps = np.asarray(m2_conv_w[0]).reshape(-1, P, 3).transpose(1, 0, 2)
    bias = columns(m2_conv_b[0])
    gain = columns(m2_norm_g[0])
    skip = np.repeat(np.asarray(m2_d[0]).reshape(HEADS // 2, 2), HD, axis=1).T
    par = []
    for g in range(NG):
        own = [DI // P + g, DI // P + NG + g] + [XB * g + k for k in range(XB)]
        here = slice(XB * g, XB * g + XB)
        par.append(np.concatenate([taps[:, own].reshape(P, -1), bias[:, own], gain[:, here], skip[:, here]], 1))
    arrays = {
        "w": w,
        "ada": ada,
        "c": np.asarray(c).reshape(D),
        "xT": np.asarray(x[0]).reshape(T, KB, P).transpose(2, 1, 0),
        "adab": columns(np.asarray(ada_b).reshape(-1)),
        "normg": np.concatenate([columns(np.asarray(norm_g).reshape(4, D)), columns(final_g)[:, None]], 1),
        "scw": np.asarray(sc_conv_w[0]).reshape(KB, P, 3).transpose(1, 0, 2),
        "par": np.stack(par, 1),
        "dtb": np.asarray(m2_dt_bias[0]).reshape(P, 1),
        "alog": np.asarray(m2_a_log[0]).reshape(P, 1),
    }
    arrays = {k: np.ascontiguousarray(v) for k, v in arrays.items()}
    nc = bacc.Bacc("TRN2", target_bir_lowering=False, num_devices=1, dynamic_dma_scratch_size=4096)
    ins = {k: nc.dram_tensor("in_" + k, v.shape, F32, kind="ExternalInput").ap() for k, v in arrays.items()}
    out = nc.dram_tensor("out", (P, KB, T), F32, kind="ExternalOutput").ap()
    cum_d = nc.dram_tensor("running_sums", (2, NG, HG, T), F32, kind="Internal").ap()
    build(nc, out=out, cum_d=cum_d, **ins)
    r = run_bass_kernel_spmd(nc, [{"in_" + k: v for k, v in arrays.items()}], core_ids=[0])
    got = r.results[0]["out"]
    return np.ascontiguousarray(got.transpose(2, 1, 0).reshape(1, T, D))
```

```python
from contextlib import ExitStack

import numpy as np

import concourse.bass as bass
from concourse import mybir

P = 128
D = 2048
T = 256
KB = D // P
DI = 4096
HEADS = 64
HD = 64
NG = 8
N = 128
FF = 4 * D
EPS = 1e-6
HG = HEADS // NG
XB = DI // NG // P
HALF = KB // 2 * P

F32 = mybir.dt.float32
F32R = mybir.dt.float32r
ALU = mybir.AluOpType
ACT = mybir.ActivationFunctionType

U_CONV = 0
U_SCOUT = U_CONV + 3 * KB
U_MLP0 = U_SCOUT + KB
U_DT = U_MLP0 + 2 * FF // P
GU = 2 + 2 * XB
U_GA = U_DT + 1
GA = 5
U_OUT0 = U_GA + GA * GU
U_GB = U_OUT0 + KB
U_OUT1 = U_GB + (NG - GA) * GU
U_MLP1 = U_OUT1 + KB
UNITS = U_MLP1 + 2 * FF // P
ADA = 4 * 3 * KB
ADA_FIRST = 2 * KB


DT_AV, DT_TOK, DT_CUM, DT_ALL = 11, 13, 14, 15


class At:

    def __init__(self, c, terms=()):
        self.c, self.terms = c, tuple(terms)

    def __add__(self, k):
        if isinstance(k, At):
            return At(self.c + k.c, self.terms + k.terms)
        return At(self.c + k, self.terms)

    def __sub__(self, k):
        return self + (-k)

    def __mul__(self, k):
        return At(self.c * k, [(r, a * k) for r, a in self.terms])

    def __floordiv__(self, k):
        assert all(a % k == 0 for _, a in self.terms)
        return At(self.c // k, [(r, a // k) for r, a in self.terms])

    def __mod__(self, k):
        assert all(a % k == 0 for _, a in self.terms)
        return self.c % k

    @property
    def v(self):
        out = self.c
        for r, a in self.terms:
            out = r * a + out
        return out


def at_least(e, sem, n):
    if isinstance(n, At):
        if not n.terms and n.c <= 0:
            return
        assert n.c > 0 or not n.terms, n.c
        n = n.v
    if isinstance(n, int) and n <= 0:
        return
    e.wait_ge(sem, n)


def first_unit(g):
    if not g.terms and g.c >= GA:
        return At(U_GB + (g.c - GA) * GU)
    return g * GU + U_GA


def blocks(g):
    return bass.ds((g * XB).v if g.terms else g.c * XB % KB, XB)


def loop(e, n, body):
    if n == 1:
        body(At(0))
    elif n > 1:
        with e.Fori(0, n) as i:
            body(At(0, [(i, 1)]))


def adas(n, ada_at, a):
    out, k = [], 0
    for s in range(n):
        out.append(a + k if s in ada_at else None)
        k += s in ada_at
    return out


def build(nc, w, ada, c, xT, adab, normg, scw, par, dtb, alog, out, cum_d):
    with ExitStack() as ctx:
        def sb(name, shape, dt=F32):
            return ctx.enter_context(nc.sbuf_tensor(name, shape, dt))

        def sem(name):
            return ctx.enter_context(nc.semaphore(name))

        x = sb("x", [P, KB, T])
        hcat = sb("hcat", [P, KB, 2 * T], F32R)
        hid = sb("hid", [P, KB, 2 * T], F32R)
        raw = sb("raw", [P, 4, HALF])
        wh = sb("wh", [P, 4, HALF], F32R)
        wl = sb("wl", [P, 4, HALF], F32R)
        adat = sb("adat", [P, 2, D])
        cond = sb("cond", [P, D])
        ta = sb("ta", [P, 2, T])
        tt = sb("tt", [P, 2, T])
        acc = sb("acc", [P, 2, T])
        th = sb("th", [P, 2, T])
        pad = sb("pad", [P, 2, T + 2])
        normt = sb("normt", [P, 6 * T])
        hv = normt[:, 0:4 * T].rearrange("p (k t) -> p k t", k=4)
        sq = normt[:, 4 * T:6 * T].rearrange("p (k t) -> p k t", k=2)
        ss = sb("ss", [P, T])
        rbc = sb("rbc", [P, T])
        modt = sb("modt", [P, 2])
        modc = sb("modc", [P, ADA])
        modb = sb("modb", [P, ADA])
        mods = sb("mods", [P, 4, 3, KB])
        ng_c = sb("ng_c", [P, 5, KB])
        scw_c = sb("scw_c", [P, KB, 3])
        parall = sb("parall", [P, NG, 32])
        parg = sb("parg", [P, 2, 32])
        dcol = sb("dcol", [P, 4])
        epsc = sb("epsc", [P, 2])
        ones = sb("ones", [P, P])
        ident = sb("ident", [P, P])
        upf = sb("upf", [P, P])
        upb = sb("upb", [P, P])
        dtS = sb("dtS", [P, 2, 2, HEADS])
        ncS = sb("ncS", [P, 2, 2, HEADS])
        dec = sb("dec", [P, 2, 4, 3 * P])
        bT = sb("bT", [P, T])
        cT = sb("cT", [P, T])
        xs = sb("xs", [P, 2, XB, T])
        zs = sb("zs", [P, 2, XB, T])
        gf = sb("gf", [P, 3 * P])
        gb = sb("gb", [P, 3 * P])
        xd = sb("xd", [P, 2, 2, HG * HD])
        em = [None, normt[:, :].rearrange("p (k t) -> p k t", k=4), dec[:, 0], dec[:, 1]]
        em.append(em[1])
        dtr, avr, dte = xd[:, 0, 0, 0:T], xd[:, 0, 1, 0:T], xd[:, 0, 0, T:2 * T]
        avS = xd[:, 1, 0, 0:T].rearrange("p (c r) -> p c r", c=2)
        ytok = xd[:, 0]
        dgrp = sb("dgrp", [P, 2, 2, HG])
        ngrp = sb("ngrp", [P, 2, 2, HG])

        psm = [ctx.enter_context(nc.psum_tensor(f"psm{i}", [P, 2 * T], F32)) for i in range(2)]
        psy = [ctx.enter_context(nc.psum_tensor(f"psy{i}", [P, 512], F32)) for i in range(2)]
        psr = [ctx.enter_context(nc.psum_tensor(f"psr{i}", [P, 512], F32)) for i in range(4)]

        raw_in = [sem(f"raw_in{i}") for i in range(4)]
        ada_in = [sem(f"ada_in{i}") for i in range(4)]
        small_in, x_in, c_in, out_done = sem("small_in"), sem("x_in"), sem("c_in"), sem("out_done")
        hi_done, lo_done, mm_done = sem("hi_done"), sem("lo_done"), sem("mm_done")
        copied, summed, stored = sem("copied"), sem("summed"), sem("stored")
        copied_a, summed_a = sem("copied_a"), sem("summed_a")
        ada_done, mod_copied, mods_done, gates_done, consts, silu_c = sem("ada_done"), sem("mod_copied"), sem("mods_done"), sem("gates_done"), sem("consts"), sem("silu_c")
        pads, halved = sem("pads"), sem("halved")
        sq_done, ss_added, ss_zero, norm_sum = sem("sq_done"), sem("ss_added"), sem("ss_zero"), sem("norm_sum")
        rms_done, eps_in = sem("rms_done"), sem("eps_in")
        hv_done, h_full, hhi_done = sem("hv_done"), sem("h_full"), sem("hhi_done")
        hlo_even, hlo_odd = sem("hlo_even"), sem("hlo_odd")
        sc_mid, sc_step, sc_conv, sc_gated, sc_hi = (sem(n) for n in ("sc_mid", "sc_step", "sc_conv", "sc_gated", "sc_hi"))
        relu_done, relu_hi = sem("relu_done"), sem("relu_hi")
        dt_act, dt_dve, dt_pe = sem("dt_act"), sem("dt_dve"), sem("dt_pe")
        cum_out, cb_in = sem("cum_out"), [sem(f"cb_in{i}") for i in range(3)]
        par_in, grp_in = sem("par_in"), sem("grp_in")
        mc_mid, mc_step, mc_conv, tanh_done = sem("mc_mid"), sem("mc_step"), sem("mc_conv"), sem("tanh_done")
        sg_scores, sg_xt, g_ready, xd_ready = sem("sg_scores"), sem("sg_xt"), sem("g_ready"), sem("xd_ready")
        g_copied, seg_done, exp_done = sem("g_copied"), sem("seg_done"), sem("exp_done")
        em_ready, y_head = sem("em_ready"), sem("y_head")
        y_tok, y_back, v_done, vz_done, gsq = sem("y_tok"), sem("y_back"), sem("v_done"), sem("vz_done"), sem("gsq")
        gss, gsum, grms, gu = sem("gss"), sem("gsum"), sem("grms"), sem("gu")
        u_hi, u_lo = sem("u_hi"), sem("u_lo")
        fin, silu_mul = sem("fin"), sem("silu_mul")
        xt_copied, mod0_mid, mod0_done = sem("xt_copied"), sem("mod0_mid"), sem("mod0_done")
        rinv, grinv, seg_far = sem("rinv"), sem("grinv"), sem("seg_far")

        block = ctx.enter_context(nc.Block())

        def walk(e, conv, gated, relu, dt, group, half_outs, scan, norm, gate=lambda n, part=None: None,
                 lead=False):
            def bodies(n, f, peel=lead):
                if peel:
                    f(At(0), True)
                    if n > 1:
                        with e.Fori(0, n - 1) as i:
                            f(At(1, [(i, 1)]), False)
                else:
                    loop(e, n, lambda i: f(i, False))

            norm(0)
            bodies(KB // 2, lambda i, f: conv(i * 6 + U_CONV, i * 2, (0, 1, 3, 4), i * 4 + ADA_FIRST, f), True)
            a = ADA_FIRST + 4 * KB // 2
            gate(0)
            bodies(4, lambda i, f: gated(i * 4 + U_SCOUT, 0, i * 4, range(4), i * 4 + a, f, True, None))
            a += KB

            norm(1)
            def up0(i, f):
                relu(i * 8 + U_MLP0, i * 8, i * 8, 1, (0, 1, 2), i * 6 + a, f)
                relu(i * 8 + (U_MLP0 + 4), i * 8 + 4, i * 8 + 4, 1, (0, 1, 2), i * 6 + (a + 3), False)
            bodies(2, up0)
            a += 12
            gate(1, slice(0, KB // 2))
            bodies(2, lambda i, f: gated(i * 4 + (U_MLP0 + KB), 1, i * 4, (0, 2), i * 2 + a, f, False, At(U_MLP0)))
            a += 4
            gate(1, slice(KB // 2, KB))
            bodies(2, lambda i, f: gated(i * 4 + (U_MLP0 + KB + 8), 1, i * 4 + 8, (), None, False, False, None),
                   False)

            def quarter0(q, aq, tiles, last):
                u, n = q * 32 + U_MLP0, len(tiles)

                def up(i, k):
                    relu(u + i * 8 + k, i * 8 + k, q * 16 + i * 8 + k, 1, tiles, aq + i * (2 * n) + n * k // 4, False)

                def down(i, k, f):
                    gated(u + i * 8 + (KB + k), 1, i * 8 + k, tiles, aq + i * (2 * n) + (4 * n + n * k // 4), f, last, u)
                loop(e, 2, lambda i: [up(i, k) for k in (0, 4)])
                bodies(2, lambda i, f: [down(i, k, f and k == 0) for k in (0, 4)])
            with e.Fori(0, 2) as q:
                q1 = At(1, [(q, 1)])
                quarter0(q1, q1 * 16 + (a - 16), (0, 2), False)
            a += 32
            quarter0(At(3), At(a), (0, 1, 2), True)
            a += 24

            norm(2)
            dt()

            def g_unit(g):
                return first_unit(g), (4, 5, 8), g * 3 + a
            group(At(0), *g_unit(At(0)))
            with e.Fori(0, 2) as i:
                for k in (1, 2):
                    g = At(k, [(i, 2)])
                    group(g, *g_unit(g))
            gate(2)
            ao = a + 3 * GA
            bodies(4, lambda i, f: gated(i * 4 + U_OUT0, 2, i * 4, (0, 2), i * 2 + ao, f, False, "chunk 0"))
            a += 8
            for k in range(GA, NG):
                group(At(k), *g_unit(At(k)))
            a += 3 * NG
            for i in range(8):
                half_outs(At(U_OUT1 + i), At(2 * i), 0, At(a + i // 2) if i % 2 == 0 else None, i, False)
            a += 4
            scan(At(NG - 1))
            for i in range(4):
                half_outs(At(U_OUT1 + 8 + i), At(2 * i), KB // 2, At(a + i), None, i == 0)
            a += 4
            loop(e, 2, lambda i: [half_outs(i * 2 + (U_OUT1 + 12 + k), i * 4 + (8 + 2 * k), KB // 2, None, None, False)
                                  for k in range(2)])

            norm(3)
            assert a == ADA
            bodies(4, lambda i, f: relu(i * 4 + U_MLP1, i * 4, i * 4 + 64, 3, (), None, f))
            gate(3)
            bodies(4, lambda i, f: gated(i * 4 + (U_MLP1 + KB), 3, i * 4, (), None, f, False, At(U_MLP1)))
            with e.Fori(0, 2) as q:
                q = At(1, [(q, 1)])
                u = q * 32 + U_MLP1
                loop(e, 4, lambda i: relu(u + i * 4, i * 4, q * 16 + i * 4 + 64, 3, (), None, False))
                bodies(4, lambda i, f: gated(u + i * 4 + KB, 3, i * 4, (), None, f, False, u))
            u = At(U_MLP1 + 96)
            loop(e, 4, lambda i: relu(u + i * 4, i * 4, i * 4 + 112, 3, (), None, False))
            bodies(3, lambda i, f: gated(u + i * 4 + KB, 3, i * 4, (), None, f, True, u))
            gated(u + (KB + 12), 3, At(12), (), None, False, True, u)
            norm(4)

        AHEAD = [(y_head, HG), (y_tok, 2), (y_back, 1), (v_done, XB), (grms, 1), (gu, XB), (u_lo, 1)]

        BLOCK_AT = [min(max(8 + k, 2 * k + 2), ADA_FIRST - 1) for k in range(KB)]
        blocks_at = lambda a: [k for k in range(KB) if BLOCK_AT[k] == a]
        halves_at = {16: 0, 18: 1, 20: 2, 22: 3}

        def first_slot(k):
            return adat[:, k, :] if k < 2 else (xs, zs)[k - 2][:, :, :, :].rearrange("p a b t -> p (a b t)")

        @block.sync
        def _(sp):
            def load_half(h):
                if not h.terms and h.c >= 2 * UNITS:
                    return
                at_least(sp, lo_done, h - 3)
                sp.dma_start(raw[:, h % 4, :], w[h.v]).then_inc(raw_in[h % 4], 16)

            def load_ada(a):
                if not a.terms and a.c >= ADA:
                    return
                at_least(sp, ada_done, a - 1)
                sp.dma_start(adat[:, a % 2, :], ada[a.v]).then_inc(ada_in[a % 2], 16)

            def load_first(a):
                at_least(sp, ada_done, a - 3)
                sp.dma_start(first_slot(a % 4), ada[a.v]).then_inc(ada_in[a % 4], 16)

            sp.dma_start(cond[:, :], c.partition_broadcast(P)).then_inc(c_in, 16)
            for a in range(4):
                load_first(At(a))
            sp.dma_start(x[:, :, :], xT).then_inc(x_in, 16)
            for src, dst in ((adab, modb[:, :]), (normg, ng_c[:, :, :]), (scw, scw_c[:, :, :]),
                             (par, parall[:, :, :]), (dtb, dcol[:, 0:1]), (alog, dcol[:, 1:2])):
                sp.dma_start(dst, src).then_inc(small_in, 16)
            for a in range(4, ADA_FIRST):
                load_first(At(a))
                if a + 4 in halves_at:
                    load_half(At(halves_at[a + 4]))
            for h in range(4, 8):
                load_half(At(h))
            load_ada(At(ADA_FIRST))
            load_ada(At(ADA_FIRST + 1))

            def steps(u, n, ada_at, a):
                k = 0
                for s in range(n):
                    load_half((u + s) * 2 + 8)
                    load_half((u + s) * 2 + 9)
                    if s in ada_at:
                        load_ada(a + (k + 2))
                        k += 1

            def load_sums(g, piece):
                if piece == 1:
                    sp.wait_ge(cum_out, 16)
                    sp.wait_ge(dt_dve, DT_ALL)
                at_least(sp, y_head, g * HG + HG + (2 if piece == 4 else 0))
                src = cum_d.rearrange("d g h t -> g d h t")[g.v][:, 2 * piece - 2:2 * piece, :]
                for d in range(2):
                    sp.dma_start(em[piece][:, 2 * d:2 * d + 2, 0:T], src[d].partition_broadcast(P))\
                        .then_inc(cb_in[piece % 3], 16)

            def scan_loads(g, s):
                for piece in {0: (3,), 2: (4,)}.get(s, ()):
                    load_sums(g, piece)

            def group(g, u, ada_at, a):
                tiles = adas(GU, ada_at, a)
                for s in range(GU):
                    if g.terms or g.c:
                        scan_loads(g - 1, s)
                    if s == (GU - 3 if g.terms or g.c else GU - 1):
                        load_sums(g, 1)
                        load_sums(g, 2)
                    steps(u + s, 1, (0,) if tiles[s] else (), tiles[s])

            def half_outs(u, n, kb, tile, s, first):
                if s is not None:
                    scan_loads(At(NG - 1), s)
                steps(u, 1, (0,) if tile else (), tile)

            def scan(g):
                pass

            def norm(n):
                if n < 4:
                    return
                for k in range(4):
                    at_least(sp, fin, 4 * (k + 1))
                    sp.dma_start(out[:, 4 * k:4 * k + 4, :], x[:, 4 * k:4 * k + 4, :]).then_inc(out_done, 16)
                sp.wait_ge(out_done, 64)

            walk(sp, lambda u, j, ada_at, a, f: steps(u, 6, ada_at, a),
                 lambda u, layer, n, ada_at, a, f, last, src: steps(u, 4, ada_at, a),
                 lambda u, j, r, layer, ada_at, a, f: steps(u, 4, ada_at, a),
                 lambda: steps(At(U_DT), 1, (), None),
                 group, half_outs, scan, norm)

        @block.gpsimd
        def _(pool):
            pool.memset(ones[:, :], 1.0).then_inc(consts, 1)
            pool.memset(ident[:, :], 0.0).then_inc(consts, 1)
            pool.memset(ss[:, :], 0.0).then_inc(ss_zero, 1)
            pool.memset(epsc[:, :], EPS).then_inc(eps_in, 1)
            pool.wait_ge(consts, 2)
            pool.affine_select(out=ident[:, :], in_=ident[:, :], compare_op=ALU.not_equal, fill=1.0, base=0,
                               pattern=[[-1, P]], channel_multiplier=1).then_inc(consts, 1)
            pool.affine_select(out=upf[:, :], in_=ones[:, :], compare_op=ALU.is_ge, fill=0.0, base=0,
                               pattern=[[1, P]], channel_multiplier=-1).then_inc(consts, 1)
            pool.affine_select(out=upb[:, :], in_=ones[:, :], compare_op=ALU.is_ge, fill=0.0, base=0,
                               pattern=[[-1, P]], channel_multiplier=1).then_inc(consts, 1)
            for s, n in AHEAD:
                pool.sem_inc(s, n)

            def keep(a):
                if a is not None:
                    at_least(pool, ada_done, a + 1)
                    pool.tensor_copy(modc[:, bass.ds(a.v, 1)], modt[:, a % 2:a % 2 + 1]).then_inc(mod_copied, 1)

            def add_square(m):
                at_least(pool, sq_done, m + 1)
                at_least(pool, ss_added, m)
                pool.tensor_tensor(ss[:, :], ss[:, :], sq[:, m % 2, :], ALU.add).then_inc(ss_added, 1)

            def conv(u, j, ada_at, a, f):
                tiles = adas(6, ada_at, a)
                for k in range(2):
                    jj, v = j + k, u + 3 * k
                    at_least(pool, summed, v + 2)
                    pool.wait_ge(pads, 1)
                    pool.tensor_tensor(pad[:, k, 1:T + 1], tt[:, v % 2, :], tt[:, (v + 1) % 2, :],
                                       ALU.mult).then_inc(stored, 2)
                    at_least(pool, summed, v + 3)
                    at_least(pool, sc_conv, jj + 1)
                    pool.tensor_tensor(acc[:, k, :], tt[:, (v + 2) % 2, :], acc[:, k, :],
                                       ALU.mult).then_inc(sc_gated, 1)
                    at_least(pool, sc_hi, jj + 1)
                    pool.tensor_tensor(hid[:, jj.v, T:2 * T], acc[:, k, :], hid[:, jj.v, 0:T].bitcast(F32),
                                       ALU.subtract).then_inc(stored, 1)
                    for t in tiles[3 * k:3 * k + 3]:
                        keep(t)

            def gated(u, layer, n, ada_at, a, f, last, src):
                tiles = adas(4, ada_at, a)
                for s in range(4):
                    v, nn = u + s, n + s
                    at_least(pool, summed, v + 1)
                    at_least(pool, stored, v)
                    pool.tensor_tensor(x[:, nn.v, :], x[:, nn.v, :], tt[:, v % 2, :], ALU.add).then_inc(stored, 1)
                    keep(tiles[s])
                    if last:
                        add_square(nn + (layer + 1) * KB)

            def relu(u, j, r, layer, ada_at, a, f):
                tiles = adas(4, ada_at, a)
                for s in range(4):
                    v, jj = u + s, j + s
                    at_least(pool, relu_hi, r + (s + 1))
                    pool.tensor_tensor(hid[:, jj.v, T:2 * T], tt[:, v % 2, :], hid[:, jj.v, 0:T].bitcast(F32),
                                       ALU.subtract).then_inc(stored, 1)
                    keep(tiles[s])

            def dt():
                at_least(pool, summed, At(U_DT + 1))
                pool.sem_inc(stored, 1)

            def sums_out():
                pool.wait_ge(dt_dve, DT_CUM)
                pool.dma_start(cum_d.rearrange("d g h t -> (d g h) t"), hv[:, 0, :]).then_inc(cum_out, 16)

            def unit_store(g, v, s):
                at_least(pool, tanh_done, g * GU + (s + 1))
                at_least(pool, stored, v)
                par2 = g % 2
                if s < 2:
                    at_least(pool, sg_scores, g)
                    src, dst = acc[:, v % 2, :], (bT, cT)[s][:, :]
                else:
                    at_least(pool, u_lo, g)
                    if s < 2 + XB:
                        src, dst = acc[:, v % 2, :], xs[:, par2, s - 2, :]
                    else:
                        src, dst = tt[:, v % 2, :], zs[:, par2, s - 2 - XB, :]
                t = th[:, v % 2, :]
                pool.tensor_tensor(t, t, src, ALU.mult).then_inc(silu_mul, 1)
                at_least(pool, silu_mul, g * GU + (s + 1))
                pool.tensor_tensor(dst, t, src, ALU.add).then_inc(stored, 1)

            def scan_piece(g, s):
                par2 = g % 2
                flat = lambda b, lo, hi: b[:, par2, lo:hi, :].rearrange("p b t -> p (b t)")
                if s == 0:
                    at_least(pool, xt_copied, g * 2 + 2)
                    at_least(pool, grp_in, g * 2 + 2)
                    for d in (1, 0):
                        if d == 0:
                            at_least(pool, xd_ready, g * 2 + 1)
                        src, dst = (xd[:, i, :, :].rearrange("p c (h e) -> p c h e", e=HD) for i in (0, d))
                        pool.tensor_tensor(dst, src, dgrp[:, :, d, :].unsqueeze(3).to_broadcast([P, 2, HG, HD]),
                                           ALU.mult).then_inc(xd_ready, 1)
                if s == 6:
                    at_least(pool, v_done, g * XB + 2 * XB)
                    at_least(pool, stored, first_unit(g) + GU)
                    pool.tensor_tensor(flat(xs, 0, XB), flat(xs, 0, XB), flat(zs, 0, XB), ALU.mult)\
                        .then_inc(vz_done, 1)
                if s == 7:
                    at_least(pool, gsq, g + 1)
                    pool.tensor_tensor(flat(zs, 0, 2), flat(zs, 0, 2), flat(zs, 2, 4), ALU.add).then_inc(gss, 1)
                    at_least(pool, gss, g * 2 + 1)
                    pool.tensor_tensor(flat(zs, 0, 1), flat(zs, 0, 1), flat(zs, 1, 2), ALU.add).then_inc(gss, 1)

            def scan_late(g, s):
                if s == 9:
                    at_least(pool, u_hi, g + 1)
                    pool.tensor_tensor(hid[:, blocks(g), T:2 * T], xs[:, g % 2, :, :],
                                       hid[:, blocks(g), 0:T].bitcast(F32), ALU.subtract).then_inc(u_lo, 1)

            def group(g, u, ada_at, a):
                at_least(pool, gu, g * XB)
                pool.wait_ge(halved, 1)
                pool.tensor_copy(parg[:, g % 2, :], parall[:, g.v, :]).then_inc(par_in, 1)
                tiles = adas(GU, ada_at, a)
                for s in range(GU):
                    if g.terms or g.c:
                        scan_piece(g - 1, s)
                    unit_store(g, u + s, s)
                    keep(tiles[s])
                    if g.terms or g.c:
                        scan_late(g - 1, s)
                    elif s == 6:
                        sums_out()

            def half_outs(u, n, kb, tile, s, first):
                if s is not None:
                    scan_piece(At(NG - 1), s)
                for half in range(2):
                    nn = n + half
                    if half:
                        at_least(pool, summed, u + 1)
                    else:
                        at_least(pool, summed_a, u + (1 - U_OUT1))
                    if half == 0:
                        at_least(pool, stored, u)
                    ins = pool.tensor_tensor(x[:, nn.v, :], x[:, nn.v, :], tt[:, half, :], ALU.add)
                ins.then_inc(stored, 1)
                if kb and not first:
                    add_square(n + (3 * KB - 2))
                    add_square(n + (3 * KB - 1))
                keep(tile)
                if s is not None:
                    scan_late(At(NG - 1), s)

            def scan(g):
                for s in (8, 9):
                    scan_piece(g, s)
                    scan_late(g, s)

            def norm(n):
                def lo_part(k):
                    at_least(pool, hhi_done, n * KB + k + 1)
                    pool.tensor_tensor(hcat[:, k, T:2 * T], hv[:, k % 4, :], hcat[:, k, 0:T].bitcast(F32),
                                       ALU.subtract).then_inc((hlo_even, hlo_odd)[k % 2], 1)

                if n == 0:
                    for a in range(4):
                        keep(At(a))
                    pool.wait_ge(ss_zero, 1)
                    for m in range(KB):
                        add_square(At(m))
                        if m % 4 == 3:
                            keep(At(4 + m // 4))
                if n == 3:
                    add_square(At(4 * KB - 2))
                    add_square(At(4 * KB - 1))
                at_least(pool, norm_sum, n + 1)
                pool.memset(ss[:, :], 0.0).then_inc(ss_zero, 1)
                at_least(pool, ss_zero, n + 2)
                if n == 0:
                    for a in range(8, ADA_FIRST + 1):
                        if a < ADA_FIRST:
                            keep(At(a))
                        if a - 1 in halves_at:
                            h = halves_at[a - 1]
                            at_least(pool, hi_done, h + 1)
                            pool.tensor_tensor(wl[:, h, :], raw[:, h, :], wh[:, h, :].bitcast(F32),
                                               ALU.subtract).then_inc(lo_done, 1)
                        for k in blocks_at(a - 1):
                            lo_part(k)
                elif n < 4:
                    for k in range(1, KB, 2):
                        lo_part(k)

            walk(pool, conv, gated, relu, dt, group, half_outs, scan, norm)

        @block.scalar
        def _(act):
            def hi(h):
                if not h.terms and h.c >= 2 * UNITS:
                    return
                at_least(act, raw_in[h % 4], (h - h % 4) * 4 + 16)
                at_least(act, mm_done, h - 3)
                act.activation(wh[:, h % 4, :], raw[:, h % 4, :], ACT.Copy).then_inc(hi_done, 1)

            def copy(v, scale=1.0):
                at_least(act, mm_done, v * 2 + 2)
                at_least(act, summed, v - 1)
                act.activation(ta[:, v % 2, :], psm[v % 2][:, 0:T], ACT.Copy, scale=scale).then_inc(copied, 1)

            def square(m, src):
                at_least(act, ss_added, m - 1)
                act.activation(sq[:, m % 2, :], src, ACT.Square).then_inc(sq_done, 1)

            def step(v, scale=1.0):
                hi(v * 2 + 4)
                copy(v, scale)
                hi(v * 2 + 5)

            act.wait_ge(c_in, 16)
            act.activation(cond[:, :], cond[:, :], ACT.Silu).then_inc(silu_c, 1)

            def conv(u, j, ada_at, a, f):
                for k in range(2):
                    jj, v = j + k, u + 3 * k
                    step(v)
                    step(v + 1)
                    at_least(act, stored, v + 2)
                    act.activation(acc[:, k, :], pad[:, k, 1:T + 1], ACT.Copy,
                                   scale=scw_c[:, jj.v, 1:2]).then_inc(sc_mid, 1)
                    step(v + 2)
                    at_least(act, sc_gated, jj + 1)
                    act.activation(hid[:, jj.v, 0:T], acc[:, k, :], ACT.Copy).then_inc(sc_hi, 1)

            def gated(u, layer, n, ada_at, a, f, last, src):
                at_least(act, gates_done, (1, 2, 4, 5)[layer] + (layer == 1 and n.c >= KB // 2))
                for s in range(4):
                    v, nn = u + s, n + s
                    step(v, mods[:, layer, 2, bass.ds(nn.v, 1)])
                    if last:
                        at_least(act, stored, v + 1)
                        square(nn + (layer + 1) * KB, x[:, nn.v, :])

            def relu(u, j, r, layer, ada_at, a, f):
                for s in range(4):
                    v, jj = u + s, j + s
                    step(v)
                    at_least(act, relu_done, r + (s + 1))
                    act.activation(hid[:, jj.v, 0:T], tt[:, v % 2, :], ACT.Copy).then_inc(relu_hi, 1)

            def dt():
                v = At(U_DT)
                step(v)
                at_least(act, summed, v + 1)
                act.activation(dte, tt[:, v % 2, :], ACT.Abs, bias=dcol[:, 0:1]).then_inc(dt_act, 1)
                act.wait_ge(dt_act, 1)
                act.activation(dte, dte, ACT.Exp, scale=-1.0).then_inc(dt_act, 1)
                act.activation(dcol[:, 2:3], dcol[:, 1:2], ACT.Exp).then_inc(dt_act, 1)

            def dt_log():
                act.wait_ge(dt_dve, 1)
                act.activation(hv[:, 0, :], hv[:, 1, :], ACT.Ln).then_inc(dt_act, 1)

            def unit(g, v, s, scanning):
                conv_unit = s < 2 + XB
                if scanning:
                    scanning()
                hi(v * 2 + 4)
                if scanning and s == 3:
                    decays(g - 1, 4)
                copy(v, 1.0 if conv_unit else 0.5)
                hi(v * 2 + 5)
                par2 = g % 2
                if conv_unit:
                    at_least(act, summed, v + 1)
                    at_least(act, par_in, g + 1)
                    at_least(act, stored, v - 1)
                    act.activation(acc[:, v % 2, :], pad[:, v % 2, 1:T + 1], ACT.Identity,
                                   bias=parg[:, par2, 18 + s:19 + s],
                                   scale=parg[:, par2, 3 * s + 1:3 * s + 2]).then_inc(mc_mid, 1)
                    at_least(act, mc_conv, g * 6 + (s + 1))
                    act.activation(th[:, v % 2, :], acc[:, v % 2, :], ACT.Tanh).then_inc(tanh_done, 1)
                else:
                    at_least(act, summed, v + 1)
                    at_least(act, stored, v - 1)
                    act.activation(th[:, v % 2, :], tt[:, v % 2, :], ACT.Tanh).then_inc(tanh_done, 1)

            def decays(g, piece):
                at_least(act, seg_done, g * 4 + piece)
                act.activation(em[piece], em[piece], ACT.Exp).then_inc(exp_done, 1)

            def scan_piece(g, s):
                par2 = g % 2
                if s == 0:
                    at_least(act, sg_scores, g + 1)
                    at_least(act, y_head, g * HG + HG)
                    act.activation(gf[:, P:T], psr[0][:, P:T], ACT.Copy).then_inc(g_copied, 1)
                    act.activation(gb[:, 0:P], psr[0][:, T:T + P], ACT.Copy).then_inc(g_copied, 1)
                    decays(g, 1)
                    at_least(act, sg_xt, g + 1)
                    at_least(act, y_back, g + 1)
                    for ch in range(2):
                        act.activation(xd[:, 0, ch, :], psy[ch][:, :], ACT.Copy).then_inc(xt_copied, 1)
                if s == 5:
                    at_least(act, y_head, g * HG + 2 * HG)
                    for ch in range(2):
                        act.activation(ytok[:, ch, :], psy[ch][:, :], ACT.Copy).then_inc(y_tok, 1)
                if s == 7:
                    at_least(act, vz_done, g + 1)
                    act.activation(zs[:, par2, :, :], xs[:, par2, :, :], ACT.Square).then_inc(gsq, 1)
                if s == 9:
                    at_least(act, gsum, g + 1)
                    act.activation(rbc[:, :], psr[2][:, 0:T], ACT.Sqrt, bias=epsc[:, 0:1],
                                   scale=1.0 / (XB * P)).then_inc(grms, 1)

            def scan_late(g, s):
                par2 = g % 2
                if s in (0, 1):
                    decays(g, s + 2)
                if s == 9:
                    at_least(act, gu, g * XB + 2 * XB)
                    act.activation(hid[:, blocks(g), 0:T], xs[:, par2, :, :], ACT.Copy).then_inc(u_hi, 1)

            def group(g, u, ada_at, a):
                for s in range(GU):
                    scanning = (lambda s=s: scan_piece(g - 1, s)) if g.terms or g.c else None
                    unit(g, u + s, s, scanning)
                    if scanning:
                        scan_late(g - 1, s)
                    elif s == 0:
                        dt_log()

            def half_outs(u, n, kb, tile, s, first):
                if s is not None:
                    scan_piece(At(NG - 1), s)
                at_least(act, gates_done, 4)
                for half in range(2):
                    nn = n + half
                    hi(u * 2 + (4 + half))
                    if half == 0 and s == 3:
                        decays(At(NG - 1), 4)
                    at_least(act, mm_done, u * 2 + (1 + half))
                    if half == 0:
                        at_least(act, summed, u)
                    act.activation(ta[:, half, :], (psm[u % 2], psr[2 + (u - U_OUT1) % 2])[half][:, 0:T], ACT.Copy,
                                   scale=mods[:, 2, 2, bass.ds(nn.v, 1)]).then_inc(copied if half else copied_a, 1)
                if kb and not first:
                    at_least(act, stored, u)
                    for k in (-2, -1):
                        square(n + (k + 3 * KB), x[:, (n + k).v, :])
                if s is not None:
                    scan_late(At(NG - 1), s)

            def scan(g):
                for s in (8, 9):
                    scan_piece(g, s)
                    scan_late(g, s)

            def norm(n):
                if n == 0:
                    act.wait_ge(eps_in, 1)
                    act.wait_ge(x_in, 16)
                    for m in range(KB):
                        square(At(m), x[:, m, :])
                if n == 3:
                    at_least(act, stored, At(U_MLP1))
                    for k in (KB - 2, KB - 1):
                        square(At(3 * KB + k), x[:, k, :])
                act.activation(epsc[:, 1:2], epsc[:, 0:1], ACT.Sqrt)
                at_least(act, norm_sum, n + 1)
                act.activation(rbc[:, :], psr[2][:, 0:T], ACT.Sqrt, bias=epsc[:, 0:1],
                               scale=1.0 / D).then_inc(rms_done, 1)
                if n == 4:
                    return
                at_least(act, mods_done, 3 * n)
                for k in range(KB):
                    if n == 0:
                        for a in range(BLOCK_AT[k - 1] if k else 0, BLOCK_AT[k]):
                            if a in halves_at:
                                hi(At(halves_at[a]))
                    at_least(act, hv_done, n * KB + k + 1)
                    h, hi_out, shift = hv[:, k % 4, :], hcat[:, k, 0:T], mods[:, n, 0, k:k + 1]
                    if n and k % 2 == 0:
                        act.activation(hi_out, h, ACT.Identity, bias=shift).then_inc(hhi_done, 1)
                    else:
                        act.activation(h, h, ACT.Identity, bias=shift).then_inc(h_full, 1)
                        at_least(act, h_full, (n + 1) * KB // 2 + k // 2 + 1 if n else k + 1)
                        act.activation(hi_out, h, ACT.Copy).then_inc(hhi_done, 1)

            walk(act, conv, gated, relu, dt, group, half_outs, scan, norm)

        @block.tensor
        def _(pe):
            def unit(u, src, ready=None):
                bank = psm[u % 2]
                for half in range(2):
                    h = u * 2 + half
                    at_least(pe, lo_done, h + 1)
                    if half == 0:
                        at_least(pe, summed, u - 1)
                    for k in range(KB // 2):
                        kb = half * KB // 2 + k
                        if ready:
                            ready(kb)
                        pe.matmul(bank[:, :], wh[:, h % 4, k * P:(k + 1) * P], src[:, kb, :],
                                  start=(kb == 0), stop=(kb == KB - 1), skip_group_check=True)
                        mm = pe.matmul(bank[:, T:2 * T], wl[:, h % 4, k * P:(k + 1) * P], src[:, kb, 0:T],
                                       start=False, stop=(kb == KB - 1), skip_group_check=True)
                    mm.then_inc(mm_done, 1)

            def norm_ready(n):
                return lambda kb: at_least(pe, (hlo_even, hlo_odd)[kb % 2], (n * KB + kb) // 2 + 1)

            def pair(u, ready):
                at_least(pe, lo_done, u * 2 + 4)
                at_least(pe, summed, u)
                for kb in range(KB):
                    ready(kb)
                    for i in range(2):
                        bank, h = psm[(u + i) % 2], (u + i) * 2 + kb // (KB // 2)
                        k = kb % (KB // 2)
                        pe.matmul(bank[:, :], wh[:, h % 4, k * P:(k + 1) * P], hcat[:, kb, :],
                                  start=(kb == 0), stop=(kb == KB - 1), skip_group_check=True)
                        mm = pe.matmul(bank[:, T:2 * T], wl[:, h % 4, k * P:(k + 1) * P], hcat[:, kb, 0:T],
                                       start=False, stop=(kb == KB - 1), skip_group_check=True)
                    if kb == KB // 2 - 1:
                        mm.then_inc(mm_done, 1)
                mm.then_inc(mm_done, 3)

            def conv(u, j, ada_at, a, first):
                if first:
                    pair(u, norm_ready(0))
                for s in range(2 if first else 0, 6):
                    unit(u + s, hcat)

            def gated(u, layer, n, ada_at, a, first, last, src):
                def ready(kb):
                    if src in ("chunk 0", "chunk 1"):
                        if kb % XB == 0:
                            at_least(pe, u_lo, kb // XB + (2 if src == "chunk 0" else 2 + NG // 2))
                    elif isinstance(src, At):
                        at_least(pe, stored, src + (kb + 1))
                    else:
                        at_least(pe, stored, 3 * (kb + 1))
                for s in range(4):
                    unit(u + s, hid, ready if first and s == 0 else None)

            def relu(u, j, r, layer, ada_at, a, first):
                if first:
                    pair(u, norm_ready(layer))
                for s in range(2 if first else 0, 4):
                    unit(u + s, hcat)

            def dt():
                pair(At(U_DT), norm_ready(2))

            def dt_late(s):
                if s == 4:
                    pe.wait_ge(dt_dve, DT_AV)
                    for i, src in ((0, dtr), (1, avr)):
                        for ch in range(2):
                            mm = pe.transpose(psr[i][:, ch * P:(ch + 1) * P], src[:, ch * P:(ch + 1) * P], ident[:, :])
                    mm.then_inc(dt_pe, 1)
                if s == 6:
                    pe.wait_ge(dt_dve, DT_TOK)
                    f, b = slice(0, HEADS), slice(HEADS, P)
                    for rows, up, near, far in ((f, upf, 0, 1), (b, upb, 1, 0)):
                        pe.matmul(psr[2][rows, near * P:(near + 1) * P], avS[:, near, rows], up[:, :],
                                  start=True, stop=True, skip_group_check=True)
                        pe.matmul(psr[2][rows, far * P:(far + 1) * P], avS[:, near, rows], ones[:, :],
                                  start=False, stop=False, skip_group_check=True)
                        mm = pe.matmul(psr[2][rows, far * P:(far + 1) * P], avS[:, far, rows], up[:, :],
                                       start=False, stop=True, skip_group_check=True)
                    mm.then_inc(dt_pe, 1)
                if s == 8:
                    pe.wait_ge(dt_dve, DT_CUM)
                    for ch in range(2):
                        mm = pe.transpose(psr[3][:, ch * P:(ch + 1) * P], hv[:, 0, ch * P:(ch + 1) * P], ident[:, :])
                    mm.then_inc(dt_pe, 1)

            def scan_piece(g, s):
                par2 = g % 2
                if s == 0:
                    at_least(pe, stored, first_unit(g) + 2 + XB)
                    at_least(pe, v_done, g * XB + XB)
                    at_least(pe, dt_dve, DT_ALL)
                    for ch in range(2):
                        mm = pe.matmul(psr[0][:, ch * T:(ch + 1) * T], bT[:, ch * P:(ch + 1) * P], cT[:, :],
                                       start=True, stop=True, skip_group_check=True)
                    mm.then_inc(sg_scores, 1)
                    at_least(pe, y_tok, g * 2 + 2)
                    for ch in range(2):
                        for b in range(XB):
                            mm = pe.transpose(psy[ch][:, b * P:(b + 1) * P], xs[:, par2, b, ch * P:(ch + 1) * P],
                                              ident[:, :])
                    mm.then_inc(sg_xt, 1)
                if 2 <= s <= 5:
                    for h in (2 * (s - 2), 2 * (s - 2) + 1):
                        if h == 0:
                            at_least(pe, xd_ready, g * 2 + 2)
                        at_least(pe, em_ready, g * 4 + (s - 1))
                        mf, mb = em[s - 1][:, h % 2, :], em[s - 1][:, 2 + h % 2, :]
                        cols = slice(h * HD, (h + 1) * HD)
                        for ch, terms in ((0, ((mf, 0, 0, 0), (mb, 2 * P, 1, 0), (mb, 0, 1, 1))),
                                          (1, ((mf, P, 0, 0), (mf, 2 * P, 0, 1), (mb, P, 1, 1)))):
                            for i, (m, at, d, sc) in enumerate(terms):
                                mm = pe.matmul(psy[ch][:, cols], m[:, at:at + P], xd[:, d, sc, cols],
                                               start=(i == 0), stop=(i == 2), skip_group_check=True)
                        mm.then_inc(y_head, 1)
                if s == 6:
                    at_least(pe, y_tok, g * 2 + 4)
                    at_least(pe, g_ready, g * 4 + 4)
                    for b in range(XB):
                        for ch in range(2):
                            at = (b % 2) * T + ch * P
                            mm = pe.transpose(psr[b // 2][:, at:at + P], ytok[:, ch, b * P:(b + 1) * P],
                                              ident[:, :])
                    mm.then_inc(y_back, 1)
                if s == 9:
                    at_least(pe, gss, g * 2 + 2)
                    if g.c == NG - 1:
                        at_least(pe, summed, At(U_OUT1 + 7))
                    at_least(pe, grms, g + 1)
                    pe.matmul(psr[2][:, 0:T], ones[:, :], zs[:, par2, 0, :], start=True, stop=True,
                              skip_group_check=True).then_inc(gsum, 1)

            def group(g, u, ada_at, a):
                for s in range(GU):
                    if g.terms or g.c:
                        scan_piece(g - 1, s)
                    else:
                        dt_late(s)
                        if s == 0:
                            continue
                    unit(u + s, hcat)

            def half_outs(u, n, kb0, tile, s, first):
                if s is not None:
                    scan_piece(At(NG - 1), s)
                for half in range(2):
                    bank, h = (psm[u % 2], psr[2 + (u - U_OUT1) % 2])[half], u * 2 + half
                    at_least(pe, lo_done, h + 1)
                    at_least(pe, summed, u - 1)
                    if half and (first or s == 0):
                        at_least(pe, grms, NG + first)
                    for k in range(KB // 2):
                        kb = kb0 + k
                        if half == 0 and (first or s == 0) and kb % XB == 0:
                            at_least(pe, u_lo, kb // XB + 2 + NG // 2)
                        pe.matmul(bank[:, :], wh[:, h % 4, k * P:(k + 1) * P], hid[:, kb, :],
                                  start=(k == 0), stop=(k == KB // 2 - 1), skip_group_check=True)
                        mm = pe.matmul(bank[:, T:2 * T], wl[:, h % 4, k * P:(k + 1) * P], hid[:, kb, 0:T],
                                       start=False, stop=(k == KB // 2 - 1), skip_group_check=True)
                    mm.then_inc(mm_done, 1)

            def scan(g):
                for s in (8, 9):
                    scan_piece(g, s)

            def norm(n):
                if n == 0:
                    pe.wait_ge(consts, 5)
                at_least(pe, ss_added, KB * (n + 1))
                if n == 3:
                    at_least(pe, grms, NG + 1)
                pe.matmul(psr[2][:, 0:T], ones[:, :], ss[:, :], start=True, stop=True,
                          skip_group_check=True).then_inc(norm_sum, 1)

            walk(pe, conv, gated, relu, dt, group, half_outs, scan, norm, lead=True)

        @block.vector
        def _(dve):
            def lo(h):
                if not h.terms and h.c >= 2 * UNITS:
                    return
                at_least(dve, hi_done, h + 1)
                dve.tensor_tensor(wl[:, h % 4, :], raw[:, h % 4, :], wh[:, h % 4, :].bitcast(F32),
                                  ALU.subtract).then_inc(lo_done, 1)

            def tile(a, first=False):
                if first:
                    at_least(dve, ada_in[a % 4], (a - a % 4) * 4 + 16)
                    t = first_slot(a % 4)
                else:
                    at_least(dve, ada_in[a % 2], (a - a % 2 - ADA_FIRST) * 8 + (ADA_FIRST * 4 + 16))
                    t = adat[:, a % 2, :]
                at_least(dve, mod_copied, a - 1)
                dve.tensor_tensor_reduce(t, t, cond[:, :], 1.0, 0.0, ALU.mult, ALU.add,
                                         modt[:, a % 2:a % 2 + 1]).then_inc(ada_done, 1)

            def step(v, add, rest=None, ada=None, scanning=None):
                if scanning:
                    scanning()
                lo(v * 2 + 4)
                at_least(dve, copied, v + 1)
                add(v).then_inc(summed, 1)
                lo(v * 2 + 5)
                if rest:
                    rest()
                if ada is not None:
                    tile(ada)

            def add_tt(v):
                at_least(dve, stored, v - 1)
                return dve.tensor_tensor(tt[:, v % 2, :], ta[:, v % 2, :], psm[v % 2][:, T:2 * T], ALU.add)

            def modulation(n, which, part=slice(0, KB), sem=mods_done):
                first = 3 * KB * n + KB * which
                at_least(dve, mod_copied, first + part.stop)
                cols = slice(first + part.start, first + part.stop)
                dve.tensor_tensor(mods[:, n, which, part], modc[:, cols], modb[:, cols], ALU.add).then_inc(sem, 1)
                if which == 1:
                    at_least(dve, mods_done, 3 * n - 1)
                    dve.scalar_tensor_tensor(out=mods[:, n, 1, :], in0=mods[:, n, 1, :], scalar=1.0,
                                             in1=ng_c[:, n, :], op0=ALU.add, op1=ALU.mult).then_inc(mods_done, 1)

            dve.memset(pad[:, :, :], 0.0).then_inc(pads, 1)
            dve.wait_ge(silu_c, 1)
            for a in range(8):
                tile(At(a), True)

            def conv(u, j, ada_at, a, f):
                tiles = adas(6, ada_at, a)
                for k in range(2):
                    jj, v = j + k, u + 3 * k
                    step(v, add_tt, None, tiles[3 * k])
                    step(v + 1, add_tt, None, tiles[3 * k + 1])

                    def taps():
                        at_least(dve, sc_mid, jj + 1)
                        dve.scalar_tensor_tensor(out=acc[:, k, :], in0=pad[:, k, 0:T], scalar=scw_c[:, jj.v, 0:1],
                                                 in1=acc[:, k, :], op0=ALU.mult, op1=ALU.add).then_inc(sc_step, 1)
                        at_least(dve, sc_step, jj + 1)
                        dve.scalar_tensor_tensor(out=acc[:, k, :], in0=pad[:, k, 2:T + 2],
                                                 scalar=scw_c[:, jj.v, 2:3], in1=acc[:, k, :], op0=ALU.mult,
                                                 op1=ALU.add).then_inc(sc_conv, 1)
                    step(v + 2, add_tt, taps, tiles[3 * k + 2])

            def gate(layer, part=slice(0, KB)):
                modulation(layer, 2, part, gates_done)

            def gated(u, layer, n, ada_at, a, f, last, src):
                tiles = adas(4, ada_at, a)

                for s in range(4):
                    nn = n + s
                    gcol = mods[:, layer, 2, bass.ds(nn.v, 1)]

                    def add(v):
                        at_least(dve, stored, v - 1)
                        return dve.scalar_tensor_tensor(out=tt[:, v % 2, :], in0=psm[v % 2][:, T:2 * T], scalar=gcol,
                                                        in1=ta[:, v % 2, :], op0=ALU.mult, op1=ALU.add)
                    step(u + s, add, None, tiles[s])

            def relu(u, j, r, layer, ada_at, a, f):
                tiles = adas(4, ada_at, a)
                for s in range(4):
                    v = u + s

                    def square():
                        at_least(dve, summed, v + 1)
                        t = tt[:, v % 2, :]
                        dve.scalar_tensor_tensor(out=t, in0=t, scalar=0.0, in1=t, op0=ALU.max,
                                                 op1=ALU.mult).then_inc(relu_done, 1)
                    step(v, add_tt, square, tiles[s])

            def dt():
                v = At(U_DT)
                step(v, add_tt)

            def dt_late(s):
                def own(ins):
                    ins.then_inc(dt_dve, 1)

                y, e, e1, m, r = tt[:, U_DT % 2, :], dte, hv[:, 1, :], hv[:, 2, :], hv[:, 3, :]
                if s == 0:
                    dve.wait_ge(dt_act, 2)
                    own(dve.tensor_scalar(e1, e, 1.0, None, ALU.add))
                    dve.wait_ge(dt_dve, 1)
                    own(dve.tensor_scalar(r, e1, -1.0, None, ALU.add))
                    dve.wait_ge(dt_dve, 2)
                    own(dve.tensor_scalar(m, r, 0.0, None, ALU.is_equal))
                if s == 1:
                    dve.wait_ge(dt_dve, 3)
                    own(dve.tensor_tensor(r, r, m, ALU.add))
                    dve.wait_ge(dt_dve, 4)
                    own(dve.reciprocal(r, r))
                    dve.wait_ge(dt_dve, 5)
                    own(dve.tensor_tensor(r, r, e, ALU.mult))
                if s == 2:
                    dve.wait_ge(dt_act, 4)
                    own(dve.tensor_tensor(m, m, hv[:, 0, :], ALU.add))
                    dve.wait_ge(dt_dve, 7)
                    own(dve.tensor_tensor(r, r, m, ALU.mult))
                    own(dve.tensor_scalar(dtr, y, dcol[:, 0:1], 0.0, ALU.add, ALU.max))
                    dve.wait_ge(dt_dve, 9)
                    own(dve.tensor_tensor(dtr, dtr, r, ALU.add))
                    dve.wait_ge(dt_dve, 10)
                    own(dve.tensor_scalar(avr, dtr, dcol[:, 2:3], -1.0, ALU.mult, ALU.mult))
                if s == 4:
                    dve.wait_ge(dt_pe, 1)
                    own(dve.tensor_copy(dtS[:, :, :, :].rearrange("p c d h -> p (c d h)"), psr[0][:, 0:T]))
                    own(dve.tensor_copy(avS[:, :, :].rearrange("p c r -> p (c r)"), psr[1][:, 0:T]))
                if s == 6:
                    dve.wait_ge(dt_pe, 2)
                    own(dve.tensor_copy(hv[:, 0, :], psr[2][:, 0:T]))
                if s == 8:
                    dve.wait_ge(dt_pe, 3)
                    own(dve.tensor_scalar(ncS[:, :, :, :].rearrange("p c d h -> p (c d h)"), psr[3][:, 0:T], -1.0,
                                          None, ALU.mult))

            def unit(g, v, s, ada, scanning):
                par2 = g % 2
                if s < 2 + XB:
                    def add(v):
                        at_least(dve, mc_conv, g * 6 + (s - 1))
                        return dve.tensor_tensor(pad[:, v % 2, 1:T + 1], ta[:, v % 2, :], psm[v % 2][:, T:2 * T],
                                                 ALU.add)

                    def taps():
                        a = acc[:, v % 2, :]
                        at_least(dve, mc_mid, g * 6 + (s + 1))
                        dve.scalar_tensor_tensor(out=a, in0=pad[:, v % 2, 0:T], scalar=parg[:, par2, 3 * s:3 * s + 1],
                                                 in1=a, op0=ALU.mult, op1=ALU.add).then_inc(mc_step, 1)
                        at_least(dve, mc_step, g * 6 + (s + 1))
                        dve.scalar_tensor_tensor(out=a, in0=pad[:, v % 2, 2:T + 2],
                                                 scalar=parg[:, par2, 3 * s + 2:3 * s + 3], in1=a, op0=ALU.mult,
                                                 op1=ALU.add).then_inc(mc_conv, 1)
                    step(v, add, taps, ada, scanning)
                else:
                    def add(v):
                        at_least(dve, stored, v - 1)
                        return dve.scalar_tensor_tensor(out=tt[:, v % 2, :], in0=psm[v % 2][:, T:2 * T], scalar=0.5,
                                                        in1=ta[:, v % 2, :], op0=ALU.mult, op1=ALU.add)
                    step(v, add, None, ada, scanning)

            def masked(g, piece):
                at_least(dve, exp_done, g * 4 + piece)
                for d, scores in enumerate((gf, gb)):
                    m = em[piece][:, 2 * d:2 * d + 2, :]
                    ins = dve.tensor_tensor(m, m, scores[:, :].unsqueeze(1).to_broadcast([P, 2, 3 * P]), ALU.mult)
                ins.then_inc(em_ready, 1)

            def scan_piece(g, s):
                par2 = g % 2
                if s == 0:
                    at_least(dve, y_head, g * HG + HG)
                    at_least(dve, g_copied, g * 2 + 2)
                    for dst, at, src, up in ((gf, 0, 0, upf), (gf, T, T + P, upf), (gb, P, T + P, upb), (gb, T, 0, upb)):
                        dve.tensor_tensor(dst[:, at:at + P], psr[0][:, src:src + P], up[:, :], ALU.mult)\
                            .then_inc(g_ready, 1)
                    at_least(dve, g_ready, g * 4 + 4)
                if s <= 2:
                    masked(g, s + 1)
                if s == 3:
                    segments(g, 4)
                if s == 6:
                    at_least(dve, y_back, g + 2)
                    for b in range(XB):
                        v = xs[:, par2, b, :]
                        dve.scalar_tensor_tensor(out=v, in0=v, scalar=parg[:, par2, 28 + b:29 + b],
                                                 in1=psr[b // 2][:, (b % 2) * T:(b % 2) * T + T],
                                                 op0=ALU.mult, op1=ALU.add).then_inc(v_done, 1)
                if s == 9:
                    at_least(dve, grms, g + 2)
                    dve.reciprocal(rbc[:, :], rbc[:, :]).then_inc(grinv, 1)
                    at_least(dve, grinv, g + 1)
                    for b in range(XB):
                        v = xs[:, par2, b, :]
                        dve.scalar_tensor_tensor(out=v, in0=v, scalar=parg[:, par2, 24 + b:25 + b], in1=rbc[:, :],
                                                 op0=ALU.mult, op1=ALU.mult).then_inc(gu, 1)

            def columns_of(g):
                at_least(dve, dt_dve, DT_ALL)
                at_least(dve, xd_ready, g * 2)
                at_least(dve, seg_done, g * 4)
                for dst, src in ((ngrp, ncS), (dgrp, dtS)):
                    cols = src[:, :, :, :].rearrange("p c d (g h) -> p c d g h", g=NG)
                    dve.tensor_copy(dst[:, :, :, :], cols[:, :, :, g.v, :]).then_inc(grp_in, 1)

            def scan_late(g, s):
                if s in (0, 1):
                    segments(g, s + 2)
                if s == 3:
                    masked(g, 4)

            def segments(g, s):
                at_least(dve, cb_in[s % 3], g * 64 + (32 if s == 1 else 64) if s % 3 == 1 else g * 32 + 32)
                if s == 1:
                    at_least(dve, grp_in, g * 2 + 2)
                rows = [(d, em[s][:, 2 * d + i, :], 2 * (s - 1) + i) for d in range(2) for i in range(2)]
                for d, row, h in rows:
                    far = slice(P, T) if d == 0 else slice(0, P)
                    ins = dve.tensor_scalar(row[:, T:3 * P], row[:, far], ngrp[:, 1 - d, d, h:h + 1], 0.0,
                                            ALU.add, ALU.min)
                ins.then_inc(seg_far, 1)
                at_least(dve, seg_far, g * 4 + s)
                for d, row, h in rows:
                    ins = dve.tensor_scalar(row[:, 0:T], row[:, 0:T], ngrp[:, d, d, h:h + 1], 0.0, ALU.add, ALU.min)
                ins.then_inc(seg_done, 1)

            def group(g, u, ada_at, a):
                tiles = adas(GU, ada_at, a)
                for s in range(GU):
                    scanning = None
                    if g.terms or g.c:
                        scanning = lambda s=s: scan_piece(g - 1, s)
                    unit(g, u + s, s, tiles[s], scanning)
                    if scanning:
                        scan_late(g - 1, s)
                    else:
                        dt_late(s)
                columns_of(g)
                segments(g, 1)

            def half_outs(u, n, kb, tile_at, s, first):
                if s is not None:
                    scan_piece(At(NG - 1), s)
                for half in range(2):
                    lo(u * 2 + (4 + half))
                    if half:
                        at_least(dve, copied, u + 1)
                    else:
                        at_least(dve, copied_a, u + (1 - U_OUT1))
                        at_least(dve, stored, u)
                    dve.scalar_tensor_tensor(out=tt[:, half, :], in0=(psm[u % 2], psr[2 + (u - U_OUT1) % 2])[half][:, T:2 * T],
                                             scalar=mods[:, 2, 2, bass.ds((n + half).v, 1)], in1=ta[:, half, :],
                                             op0=ALU.mult, op1=ALU.add).then_inc(summed if half else summed_a, 1)
                if tile_at:
                    tile(tile_at)
                if s is not None:
                    scan_late(At(NG - 1), s)

            def scan(g):
                for s in (8, 9):
                    scan_piece(g, s)
                    scan_late(g, s)

            def norm(n):
                def whole(k):
                    if k >= 4:
                        at_least(dve, (hlo_even, hlo_odd)[k % 2], (n * KB + k - 4) // 2 + 1)
                    dve.scalar_tensor_tensor(out=hv[:, k % 4, :], in0=x[:, k, :], scalar=mods[:, n, 1, k:k + 1],
                                             in1=rbc[:, :], op0=ALU.mult, op1=ALU.mult).then_inc(hv_done, 1)

                def lo_part(k):
                    if k < 0 or k % 2:
                        return
                    at_least(dve, hhi_done, n * KB + k + 1)
                    dve.scalar_tensor_tensor(out=hcat[:, k, T:2 * T], in0=hv[:, k % 4, :],
                                             scalar=mods[:, n, 0, k:k + 1], in1=hcat[:, k, 0:T].bitcast(F32),
                                             op0=ALU.add, op1=ALU.subtract).then_inc(hlo_even, 1)

                if 0 < n < 4:
                    modulation(n, 0)
                    modulation(n, 1)
                at_least(dve, rms_done, n + 1)
                dve.reciprocal(rbc[:, :], rbc[:, :]).then_inc(rinv, 1)
                at_least(dve, rinv, n + 1)
                if n == 4:
                    for k in range(KB):
                        dve.scalar_tensor_tensor(out=x[:, k, :], in0=x[:, k, :], scalar=ng_c[:, 4, k:k + 1],
                                                 in1=rbc[:, :], op0=ALU.mult, op1=ALU.mult).then_inc(fin, 1)
                elif n:
                    at_least(dve, mods_done, 3 * n)
                    for k in range(KB + 2):
                        if k < KB:
                            whole(k)
                        lo_part(k - 2)
                else:
                    dve.wait_ge(small_in, 96)
                    for a in range(8, ADA_FIRST):
                        tile(At(a), True)
                        for k in blocks_at(a):
                            at_least(dve, mod_copied, 2 * k + 2)
                            dve.tensor_scalar(mods[:, 0, 0, k:k + 1], modc[:, 2 * k:2 * k + 1], modb[:, k:k + 1],
                                              None, ALU.add)
                            dve.tensor_scalar(mods[:, 0, 1, k:k + 1], modc[:, 2 * k + 1:2 * k + 2],
                                              modb[:, KB + k:KB + k + 1], 1.0, ALU.add, ALU.add).then_inc(mod0_mid, 1)
                            at_least(dve, mod0_mid, k + 1)
                            dve.tensor_tensor(mods[:, 0, 1, k:k + 1], mods[:, 0, 1, k:k + 1], ng_c[:, 0, k:k + 1],
                                              ALU.mult).then_inc(mod0_done, 1)
                            at_least(dve, mod0_done, k + 1)
                            whole(k)
                    dve.tensor_scalar(parall[:, :, 0:24], parall[:, :, 0:24], 0.5, None, ALU.mult)\
                        .then_inc(halved, 1)

            walk(dve, conv, gated, relu, dt, group, half_outs, scan, norm, gate)

    return nc


def kernel(x, c, ada_w, ada_b, norm_g, final_g, sc_in_w, sc_conv_w, sc_out_w, m2_in_w, m2_conv_w, m2_conv_b,
           m2_dt_bias, m2_a_log, m2_d, m2_norm_g, m2_out_w, mlp_w1, mlp_w2):
    import concourse.bacc as bacc
    from concourse.bass_utils import run_bass_kernel_spmd

    def slabs(m, order=None):
        m = np.asarray(m).reshape(2, KB // 2, P, -1, P)
        m = m.transpose(3, 0, 2, 1, 4).reshape(-1, 2, P, HALF)
        return m if order is None else m[order]

    def mlp(w1, w2):
        up, parts = slabs(w1), []
        for q in range(4):
            parts += [up[q * KB:(q + 1) * KB], slabs(w2[q * D:(q + 1) * D])]
        return parts

    conv_in = slabs(sc_in_w[0]).reshape(3, KB, 2, P, HALF)
    conv_order = np.stack([conv_in[1], conv_in[2], conv_in[0]], 1).reshape(-1, 2, P, HALF)
    m2 = slabs(m2_in_w[0])
    z0, x0 = 0, DI // P
    b0 = x0 + DI // P
    c0, dt0 = b0 + NG, b0 + 2 * NG

    def groups(lo, hi):
        return m2[[i for g in range(lo, hi) for i in
                   [b0 + g, c0 + g] + [x0 + XB * g + k for k in range(XB)] + [z0 + XB * g + k for k in range(XB)]]]
    units = [conv_order, slabs(sc_out_w[0])] + mlp(mlp_w1[0], mlp_w2[0])
    units += [m2[[dt0]], groups(0, GA), slabs(m2_out_w[0][:D]), groups(GA, NG)]
    late_out = slabs(m2_out_w[0][D:])
    units += [late_out[:, half].reshape(KB // 2, 2, P, HALF) for half in range(2)]
    units += mlp(mlp_w1[1], mlp_w2[1])
    w = np.concatenate(units).reshape(2 * UNITS, P, HALF)

    ada = np.asarray(ada_w).reshape(4, D, 3 * KB, P).transpose(0, 2, 3, 1).reshape(ADA, P, D)
    first = np.arange(ADA_FIRST).reshape(2, KB).T.reshape(-1)
    ada = ada[np.concatenate([first, np.arange(ADA_FIRST, ADA)])]

    def columns(v):
        v = np.asarray(v)
        v = v.reshape(v.shape[:-1] + (-1, P))
        return np.moveaxis(v, -1, 0)

    taps = np.asarray(m2_conv_w[0]).reshape(-1, P, 3).transpose(1, 0, 2)
    bias = columns(m2_conv_b[0])
    gain = columns(m2_norm_g[0])
    skip = np.repeat(np.asarray(m2_d[0]).reshape(HEADS // 2, 2), HD, axis=1).T
    par = []
    for g in range(NG):
        own = [DI // P + g, DI // P + NG + g] + [XB * g + k for k in range(XB)]
        here = slice(XB * g, XB * g + XB)
        par.append(np.concatenate([taps[:, own].reshape(P, -1), bias[:, own], gain[:, here], skip[:, here]], 1))
    arrays = {
        "w": w,
        "ada": ada,
        "c": np.asarray(c).reshape(D),
        "xT": np.asarray(x[0]).reshape(T, KB, P).transpose(2, 1, 0),
        "adab": columns(np.asarray(ada_b).reshape(-1)),
        "normg": np.concatenate([columns(np.asarray(norm_g).reshape(4, D)), columns(final_g)[:, None]], 1),
        "scw": np.asarray(sc_conv_w[0]).reshape(KB, P, 3).transpose(1, 0, 2),
        "par": np.stack(par, 1),
        "dtb": np.asarray(m2_dt_bias[0]).reshape(P, 1),
        "alog": np.asarray(m2_a_log[0]).reshape(P, 1),
    }
    arrays = {k: np.ascontiguousarray(v) for k, v in arrays.items()}
    nc = bacc.Bacc("TRN2", target_bir_lowering=False, num_devices=1, dynamic_dma_scratch_size=4096)
    ins = {k: nc.dram_tensor("in_" + k, v.shape, F32, kind="ExternalInput").ap() for k, v in arrays.items()}
    out = nc.dram_tensor("out", (P, KB, T), F32, kind="ExternalOutput").ap()
    cum_d = nc.dram_tensor("running_sums", (2, NG, HG, T), F32, kind="Internal").ap()
    build(nc, out=out, cum_d=cum_d, **ins)
    r = run_bass_kernel_spmd(nc, [{"in_" + k: v for k, v in arrays.items()}], core_ids=[0])
    got = r.results[0]["out"]
    return np.ascontiguousarray(got.transpose(2, 1, 0).reshape(1, T, D))
```
